# Optimizing a Trainium2 kernel written in Bass

```python
import jax, jax.numpy as jnp
from jax import lax
import numpy as np

D_MODEL = 1024
BATCH = 1
SEQ = 512
DEPTH = 2

EPS = 1e-6
CHUNK = 64
HEAD_DIM = 128
HG_HEADS = D_MODEL // 2 // HEAD_DIM
HG_DK = HEAD_DIM
HG_DV = HEAD_DIM
HG_W = HG_HEADS * HG_DK
RET_HEADS = D_MODEL // 2 // HEAD_DIM
RET_DK = HEAD_DIM
RET_DV = HEAD_DIM
RET_W = RET_HEADS * RET_DK
EVEN_SPLITS = (HG_W, HG_W, HG_HEADS * HG_DV, HG_HEADS * HG_DV,
               RET_W, RET_W, RET_HEADS * RET_DV, RET_HEADS * RET_DV)
EVEN_MIX_W = HG_HEADS * HG_DV + RET_HEADS * RET_DV
GLA_HEADS = 4
GLA_K_W = D_MODEL // 2
GLA_V_W = D_MODEL
GLA_DK = GLA_K_W // GLA_HEADS
GLA_DV = GLA_V_W // GLA_HEADS
GLA_RANK = 16
GLA_GATE_NORM = 16.0
ODD_SPLITS = (GLA_K_W, GLA_K_W, GLA_V_W, GLA_V_W, GLA_RANK)
N_EXPERTS = 16
N_GROUPS = 4
EXPERTS_PER_GROUP = N_EXPERTS // N_GROUPS
TOP_K = 2
D_EXPERT = D_MODEL // 2
ROPE_BASE = 10000.0
N_EVEN = (DEPTH + 1) // 2
N_ODD = DEPTH // 2

kernel_name = "hybrid_hgrn2_retnet_gla_grouped_moe_adaln"

def split_cols(a, sizes):
    offs = np.cumsum(sizes)[:-1]
    return jnp.split(a, [int(o) for o in offs], axis=-1)

def rmsnorm(x, w):
    xf = x.astype(jnp.float32)
    y = xf * lax.rsqrt(jnp.mean(xf * xf, axis=-1, keepdims=True) + EPS) * w.astype(jnp.float32)
    return y.astype(x.dtype)

def head_rmsnorm(o, w, n_heads):
    B_, S, W = o.shape
    oh = o.reshape(B_, S, n_heads, W // n_heads)
    oh = oh * lax.rsqrt(jnp.mean(oh * oh, axis=-1, keepdims=True) + EPS)
    return oh.reshape(B_, S, W) * w.astype(jnp.float32)

def to_heads(a, n_heads):
    B_, S, W = a.shape
    return a.reshape(B_, S, n_heads, W // n_heads).transpose(0, 2, 1, 3)

def from_heads(o):
    B_, H, S, d = o.shape
    return o.transpose(0, 2, 1, 3).reshape(B_, S, H * d)

def rotary(x):
    S, dh = x.shape[2], x.shape[3]
    inv = ROPE_BASE ** (-jnp.arange(0, dh, 2, dtype=jnp.float32) / dh)
    ang = jnp.arange(S, dtype=jnp.float32)[:, None] * inv[None, :]
    cos, sin = jnp.cos(ang), jnp.sin(ang)
    x1, x2 = x[..., : dh // 2], x[..., dh // 2:]
    return jnp.concatenate([x1 * cos - x2 * sin, x2 * cos + x1 * sin], axis=-1)

def chunk_gated_linear_attention(q, k, v, log_g):
    f32 = jnp.float32
    B_, H, S, dk = q.shape
    dv = v.shape[-1]
    n = S // CHUNK
    q = q.astype(f32).reshape(B_, H, n, CHUNK, dk)
    k = k.astype(f32).reshape(B_, H, n, CHUNK, dk)
    v = v.astype(f32).reshape(B_, H, n, CHUNK, dv)
    lg = log_g.astype(f32)
    lg = lg.reshape(lg.shape[0], H, n, CHUNK, lg.shape[-1])
    b = jnp.cumsum(lg, axis=3)
    b_last = b[:, :, :, CHUNK - 1:, :]
    b_mid = b[:, :, :, CHUNK // 2 - 1: CHUNK // 2, :]
    causal = jnp.tril(jnp.ones((CHUNK, CHUNK), dtype=bool))
    scores = jnp.einsum('bhntk,bhnsk->bhnts', q * jnp.exp(b - b_mid), k * jnp.exp(b_mid - b))
    o_intra = jnp.einsum('bhnts,bhnsv->bhntv', jnp.where(causal, scores, 0.0), v)
    q_inter = q * jnp.exp(b)
    u = jnp.einsum('bhnsk,bhnsv->bhnkv', k * jnp.exp(b_last - b), v)
    decay = jnp.exp(b_last[:, :, :, 0, :])

    def step(state, inp):
        q_c, u_c, d_c = inp
        o_c = jnp.einsum('bhtk,bhkv->bhtv', q_c, state)
        return d_c[..., None] * state + u_c, o_c

    state0 = jnp.zeros((B_, H, dk, dv), f32)
    _, o_inter = lax.scan(step, state0, (jnp.moveaxis(q_inter, 2, 0),
                                          jnp.moveaxis(u, 2, 0),
                                          jnp.moveaxis(decay, 2, 0)))
    o = o_intra + jnp.moveaxis(o_inter, 0, 2)
    return o.reshape(B_, H, S, dv)

def even_mixer(h, w_in, lb, hg_norm_w, ret_norm_w, w_out):
    f32 = jnp.float32
    S = h.shape[1]
    proj = h @ w_in
    hq, hf, hi, hg, rq, rk, rv, rg = split_cols(proj, EVEN_SPLITS)
    f = lb + (1.0 - lb) * jax.nn.sigmoid(hf.astype(f32))
    o_hg = chunk_gated_linear_attention(
        to_heads(jax.nn.sigmoid(hq.astype(f32)), HG_HEADS),
        to_heads(1.0 - f, HG_HEADS),
        to_heads(hi, HG_HEADS),
        to_heads(jnp.log(f), HG_HEADS))
    o_hg = head_rmsnorm(from_heads(o_hg), hg_norm_w, HG_HEADS) * jax.nn.silu(hg.astype(f32))
    log_gamma = jnp.log1p(-jnp.exp2(-5.0 - jnp.arange(RET_HEADS, dtype=f32)))
    log_g = jnp.broadcast_to(log_gamma[None, :, None, None], (1, RET_HEADS, S, 1))
    q_r = rotary(to_heads(rq.astype(f32), RET_HEADS))
    k_r = rotary(to_heads(rk.astype(f32), RET_HEADS)) * (RET_DK ** -0.5)
    o_ret = chunk_gated_linear_attention(q_r, k_r, to_heads(rv, RET_HEADS), log_g)
    o_ret = head_rmsnorm(from_heads(o_ret), ret_norm_w, RET_HEADS) * jax.nn.silu(rg.astype(f32))
    o = jnp.concatenate([o_hg, o_ret], axis=-1).astype(h.dtype)
    return o @ w_out

def odd_mixer(h, w_in, w_a2, b_a2, gla_norm_w, w_out):
    f32 = jnp.float32
    proj = h @ w_in
    gq, gk, gv, gg, ga = split_cols(proj, ODD_SPLITS)
    log_a = jax.nn.log_sigmoid((ga @ w_a2 + b_a2).astype(f32)) / GLA_GATE_NORM
    o = chunk_gated_linear_attention(
        to_heads(gq.astype(f32) * (GLA_DK ** -0.5), GLA_HEADS),
        to_heads(gk, GLA_HEADS),
        to_heads(gv, GLA_HEADS),
        to_heads(log_a, GLA_HEADS))
    o = head_rmsnorm(from_heads(o), gla_norm_w, GLA_HEADS) * jax.nn.silu(gg.astype(f32))
    return o.astype(h.dtype) @ w_out

def grouped_moe(h, w_router, b_router, w_gate, w_up, w_down):
    f32 = jnp.float32
    B_, S, D = h.shape
    t = h.reshape(-1, D)
    probs = jax.nn.softmax((t @ w_router).astype(f32), axis=-1)
    sel = probs + b_router.astype(f32)
    group_score = sel.reshape(-1, N_GROUPS, EXPERTS_PER_GROUP).max(axis=-1)
    group_mask = jax.nn.one_hot(jnp.argmax(group_score, axis=-1), N_GROUPS, dtype=bool)
    expert_mask = jnp.repeat(group_mask, EXPERTS_PER_GROUP, axis=-1)
    _, top_i = lax.top_k(jnp.where(expert_mask, sel, -jnp.inf), TOP_K)
    top_w = jnp.take_along_axis(probs, top_i, axis=-1)
    top_w = top_w / jnp.sum(top_w, axis=-1, keepdims=True)
    combine = jnp.sum(jax.nn.one_hot(top_i, N_EXPERTS, dtype=f32) * top_w[..., None], axis=1)

    def expert(acc, inp):
        wg, wu, wd, cw = inp
        y = (jax.nn.silu(t @ wg) * (t @ wu)) @ wd
        return acc + cw[:, None] * y.astype(f32), None

    out, _ = lax.scan(expert, jnp.zeros(t.shape, f32), (w_gate, w_up, w_down, combine.T))
    return out.astype(h.dtype).reshape(B_, S, D)

def setup_inputs(seed: int = 0) -> dict:
    key = jax.random.key(seed)
    ks = jax.random.split(key, 24)
    nrm = jax.random.normal
    D = D_MODEL
    return {
        "x": nrm(ks[0], (BATCH, SEQ, D), jnp.float32),
        "c": nrm(ks[1], (BATCH, D), jnp.float32),
        "w_ada": nrm(ks[2], (DEPTH, D, 6 * D), jnp.float32) * (0.5 * D ** -0.5),
        "b_ada": nrm(ks[3], (DEPTH, 6 * D), jnp.float32) * 0.02,
        "norm_mix_w": 1.0 + 0.05 * nrm(ks[4], (DEPTH, D), jnp.float32),
        "norm_ffn_w": 1.0 + 0.05 * nrm(ks[5], (DEPTH, D), jnp.float32),
        "w_in_even": nrm(ks[6], (N_EVEN, D, sum(EVEN_SPLITS)), jnp.float32) * D ** -0.5,
        "hg_lb_logits": 0.1 * nrm(ks[7], (DEPTH + 1, HG_W), jnp.float32),
        "hg_norm_w": 1.0 + 0.05 * nrm(ks[8], (N_EVEN, HG_HEADS * HG_DV), jnp.float32),
        "ret_norm_w": 1.0 + 0.05 * nrm(ks[9], (N_EVEN, RET_HEADS * RET_DV), jnp.float32),
        "w_out_even": nrm(ks[10], (N_EVEN, EVEN_MIX_W, D), jnp.float32) * EVEN_MIX_W ** -0.5,
        "w_in_odd": nrm(ks[11], (N_ODD, D, sum(ODD_SPLITS)), jnp.float32) * D ** -0.5,
        "w_gla_a2": nrm(ks[12], (N_ODD, GLA_RANK, GLA_K_W), jnp.float32) * GLA_RANK ** -0.5,
        "b_gla_a2": 0.02 * nrm(ks[13], (N_ODD, GLA_K_W), jnp.float32),
        "gla_norm_w": 1.0 + 0.05 * nrm(ks[14], (N_ODD, GLA_V_W), jnp.float32),
        "w_out_odd": nrm(ks[15], (N_ODD, GLA_V_W, D), jnp.float32) * GLA_V_W ** -0.5,
        "w_router": nrm(ks[16], (D, N_EXPERTS), jnp.float32) * D ** -0.5,
        "b_router": 0.01 * nrm(ks[17], (N_EXPERTS,), jnp.float32),
        "w_gate": nrm(ks[18], (DEPTH, N_EXPERTS, D, D_EXPERT), jnp.float32) * D ** -0.5,
        "w_up": nrm(ks[19], (DEPTH, N_EXPERTS, D, D_EXPERT), jnp.float32) * D ** -0.5,
        "w_down": nrm(ks[20], (DEPTH, N_EXPERTS, D_EXPERT, D), jnp.float32) * D_EXPERT ** -0.5,
        "final_norm_w": 1.0 + 0.05 * nrm(ks[21], (D,), jnp.float32),
    }

def reference(x, c, w_ada, b_ada, norm_mix_w, norm_ffn_w, w_in_even, hg_lb_logits,
              hg_norm_w, ret_norm_w, w_out_even, w_in_odd, w_gla_a2, b_gla_a2,
              gla_norm_w, w_out_odd, w_router, b_router, w_gate, w_up, w_down,
              final_norm_w):
    lb_table = jnp.cumsum(jax.nn.softmax(hg_lb_logits.astype(jnp.float32), axis=0), axis=0)
    c_act = jax.nn.silu(c)
    for l in range(DEPTH):
        mod = c_act @ w_ada[l] + b_ada[l]
        sh1, sc1, g1, sh2, sc2, g2 = jnp.split(mod[:, None, :], 6, axis=-1)
        h = rmsnorm(x, norm_mix_w[l]) * (1.0 + sc1) + sh1
        j = l // 2
        if l % 2 == 0:
            y = even_mixer(h, w_in_even[j], lb_table[l], hg_norm_w[j], ret_norm_w[j], w_out_even[j])
        else:
            y = odd_mixer(h, w_in_odd[j], w_gla_a2[j], b_gla_a2[j], gla_norm_w[j], w_out_odd[j])
        x = x + g1 * y
        h = rmsnorm(x, norm_ffn_w[l]) * (1.0 + sc2) + sh2
        x = x + g2 * grouped_moe(h, w_router, b_router, w_gate[l], w_up[l], w_down[l])
    return rmsnorm(x, final_norm_w)


_drawn_inputs = setup_inputs


def setup_inputs(seed=0):
    import zlib

    import numpy as np

    out = dict(_drawn_inputs(seed))
    spreads = {}
    factors = {'hg_lb_logits': 25.04, 'b_gla_a2': 8.0, 'gla_norm_w': 2.93}
    for name, (base, spread) in spreads.items():
        noise = np.random.default_rng([zlib.crc32(name.encode()), seed]).standard_normal(out[name].shape)
        drawn = base * np.exp(spread * noise) if base else spread * noise
        out[name] = __import__('jax').numpy.asarray(drawn.astype(out[name].dtype))
    for name, factor in factors.items():
        out[name] = (out[name] * factor).astype(out[name].dtype)
    return out
```

```python
from contextlib import ExitStack

import numpy as np

import concourse.bass as bass
from concourse import mybir

F32 = mybir.dt.float32
U32 = mybir.dt.uint32
U8 = mybir.dt.uint8
ALU = mybir.AluOpType
ACT = mybir.ActivationFunctionType
AX = mybir.AxisListType.X

P = 128
D = 1024
S = 512
DEPTH = 2
EPS = 1e-6
NT = S // P
KD = D // P
CHUNK = 64
NCH = S // CHUNK
HEADS = 4
E = 16
GROUPS = 4
EPG = E // GROUPS
DE = D // 2
KE = DE // P
UNIT = 8 * 512
NADA = 6 * D // 512
MAXOVER = 8
NLIST = E + MAXOVER + 2
GLA_RANK = 16
BIG = 100.0

CONST_WIDTHS = [("ident", 128), ("ones", 128), ("tri", 128), ("scanmask", 512), ("cos", 512), ("sin", 512),
                ("gamrow", 4 * 128), ("decay", 4 * 128), ("kdecay", 4), ("tokid", 4), ("iota_e", 16),
                ("iota_e_big", 16), ("iota_g_big", 4), ("iota_j", 8), ("eps", 1)]
CONST_AT = {}
NCONST = 0
for _name, _w in CONST_WIDTHS:
    CONST_AT[_name] = (NCONST, NCONST + _w)
    NCONST += _w


def gamma_powers():
    f32 = np.float32
    lg = np.log1p(-np.exp2(f32(-5.0) - np.arange(HEADS, dtype=f32))).astype(f32)
    return lg.astype(np.float64)


def constants():
    f32 = np.float32
    c = np.zeros((P, NCONST), f32)

    def put(name, v):
        a, b = CONST_AT[name]
        c[:, a:b] = v

    p = np.arange(P)
    t = np.arange(S)
    put("ident", np.eye(P))
    put("ones", 1.0)
    put("tri", (p[:, None] < p[None, :]))
    put("scanmask", (t % CHUNK != 0)[None, :])
    half = P // 2
    inv = f32(10000.0) ** (-np.arange(0, P, 2, dtype=f32) / f32(P))
    ang = (np.arange(S, dtype=f32)[:, None] * inv[None, :].astype(f32)).astype(f32)
    put("cos", np.cos(ang).T[p % half])
    put("sin", np.sin(ang).T[p % half] * np.where(p < half, -1.0, 1.0)[:, None])
    lg = gamma_powers()
    scale = float(P) ** -0.5
    put("gamrow", np.concatenate([np.exp(lg[h] * (p + 1)) for h in range(HEADS)])[None, :])
    dist = p[None, :] - p[:, None]
    put("decay", np.concatenate([np.where(dist >= 0, np.exp(lg[h] * dist) * scale, 0.0) for h in range(HEADS)], 1))
    put("kdecay", np.stack([np.exp(lg[h] * (P - 1 - p)) * scale for h in range(HEADS)], 1))
    put("tokid", p[:, None] + P * np.arange(NT)[None, :])
    put("iota_e", np.arange(E)[None, :])
    put("iota_e_big", np.arange(E)[None, :] + BIG)
    put("iota_g_big", np.arange(GROUPS)[None, :] + BIG)
    put("iota_j", np.arange(MAXOVER)[None, :])
    put("eps", EPS)
    s = p[:, None]
    tt = p[None, :]
    m = ((s // CHUNK == tt // CHUNK) & (s <= tt)).astype(f32)
    return c, np.tile(m, (1, NT))


def schedule():
    phases = []
    st = [("ada", a) if k == 0 else ("adacol", a) for a in range(4) for k in range(2)]
    st.append(("norm", 0))
    nxt = [4]

    def adas(count):
        out = []
        first = nxt[0]
        pend = [a for a in range(first - 2, first) if a >= 4]
        out += [("adacol", a) for a in pend]
        out += [("ada", a) for a in range(first, first + count)]
        nxt[0] += count
        return out

    ret = [(s_, "ret", h) for h in range(HEADS) for s_ in ("prep", "A", "B", "C", "D")]
    hg = [("prep", "hg", 0)]
    for h in range(HEADS):
        hg += [("A", "hg", h)]
        if h + 1 < HEADS:
            hg += [("prep", "hg", h + 1)]
        hg += [("B", "hg", h), ("C", "hg", h), ("D", "hg", h)]
    core = ret + hg
    for kind in ("rq", "rk", "rv"):
        st += [("proj", kind, g) for g in range(4)] + adas(2)

    def take(n):
        out = []
        while n and core:
            out.append(core.pop(0))
            if out[-1][0] != "prep":
                n -= 1
        return out

    for kind, n in (("hf", 1), ("hq", 1), ("hi", 1), ("rg", 2), ("hg", 2)):
        if kind == "rg":
            while core and core[0][1] == "ret":
                st += take(1)
        for g in range(4):
            st.append(("proj", kind, g))
            if kind == "hg":
                continue
            st += take(n)
        if kind == "rg":
            st += take(99)
        st += adas(2)
    st.append(("gb", 0))
    st += [("proj", "wo0", g) for g in range(4)] + adas(2)
    st += [("proj", "wo1", g) for g in range(4)] + adas(2)
    st += [("adacol", a) for a in range(nxt[0] - 2, nxt[0])]
    assert nxt[0] == 2 * NADA, nxt
    phases.append(st)
    st = [("norm", 2), ("low", 0)]
    core = []
    core += [("prep", "gla", 0)]
    for h in range(HEADS):
        core += [("A", "gla", h)]
        if h + 1 < HEADS:
            core += [("prep", "gla", h + 1)]
        core += [("B", "gla", h), ("C", "gla", h), ("D", "gla", h)]
    for kind in ("gq", "gk", "gv0", "gv1"):
        st += [("proj", kind, g) for g in range(4)]
        if kind == "gk":
            st += [core.pop(0)]
    for kind in ("gg0", "gg1"):
        need = 2 if kind == "gg0" else 4
        while any(c[0] != "prep" and c[2] < need for c in core):
            st += [core.pop(0)]
        for g in range(4):
            st.append(("proj", kind, g))
            for _ in range(3):
                if core and kind == "gg0":
                    st.append(core.pop(0))
    st.append(("gb", 2))
    st += [("proj", "wo0", g) for g in range(4)] + [("proj", "wo1", g) for g in range(4)]
    phases.append(st)
    return phases


def number(phases):
    seen = {}
    out = []
    for st in phases:
        ph = []
        for step in st:
            kind = step[0]
            ph.append((step, seen.get(kind, 0)))
            seen[kind] = seen.get(kind, 0) + 1
        out.append(ph)
    return out


GATES = {"hg": 0, "rg": 4, "gg0": 0, "gg1": 4}
FILLS = {"ret": [[0, 1, 2]], "hg": [[0, 1, 2, 3, 4, 5, 6]], "gla": [[0, 1, 2, 3], [4, 5, 6]]}


def update_at(what, c):
    if what == "ret":
        return 4, c * P
    return 4 + c % 2, (c // 2 * P if what == "hg" else c % 4 // 2 * 2 * P)




def fills_before(n):
    return sum(len(FILLS[("ret", "hg", "gla")[h // HEADS]]) for h in range(n))


def rot_index(name, g):
    return g + (HEADS if name == "rk" else 0)


W_COLS = {"hq": 0, "hf": 1, "hi": 2, "hg": 3, "rq": 4, "rk": 5, "rv": 6, "rg": 7,
          "gq": 0, "gk": 1, "gv0": 2, "gv1": 3, "gg0": 4, "gg1": 5}


def ring_units(phases):
    out = []
    for layer, st in enumerate(phases):
        units = []
        for step in st:
            u = ("ada", step[1]) if step[0] == "ada" else ("w", step[1]) if step[0] == "proj" else None
            if u and u not in units:
                units.append(u)
        out.append(units)
    return out


class Chain:

    def __init__(self, eng, sem):
        self.eng, self.sem, self.n = eng, sem, 0

    def add(self, ins):
        ins.then_inc(self.sem, 1)
        self.n += 1

    def wait(self):
        self.eng.wait_ge(self.sem, self.n)

    def link(self, ins):
        self.add(ins)
        self.wait()


def keep(eng, reg, value):
    eng.reg_mov(reg, value)
    return eng.snap(reg)


def trunk(nc, x, c, w_ada, b_ada, norm_mix_w, norm_ffn_w, w_in_even, hg_lb_logits, hg_norm_w, ret_norm_w,
          w_out_even, w_in_odd, w_gla_a2, b_gla_a2, gla_norm_w, w_out_odd, w_router, b_router, w_gate, w_up,
          w_down, final_norm_w, consts, cmask, out):
    phases = number(schedule())
    units = ring_units(schedule())
    gamma = np.exp(gamma_powers() * P)

    with ExitStack() as ctx:
        def sb(name, shape, dt=F32):
            return ctx.enter_context(nc.sbuf_tensor(name, shape, dt))

        def sem(name):
            return ctx.enter_context(nc.semaphore(name))

        def dram(name, shape, dt=F32):
            return nc.dram_tensor(name, shape, dt, kind="Internal").ap()

        ring = sb("ring", [P, 6, UNIT])
        X = sb("X", [P, NT, D])
        HT = sb("HT", [P, KD, S])
        OT = sb("OT", [P, KD, S])
        XN = OT[:, :, :].rearrange("p k s -> p (k s)").rearrange("p (t d) -> p t d", t=NT)
        MX = sb("MX", [P, 6 * 2048])
        SC = ring[:, 4:6, :].rearrange("p a b -> p (a b)")
        C = sb("C", [P, NCONST])
        CM = sb("CM", [P, S], U8)
        VC = sb("VC", [P, 168])
        MOD = sb("MOD", [P, 2 * 48])
        AM = sb("AM", [P, 4, KD])
        WR = sb("WR", [P, KD, E])
        BR = sb("BR", [P, E])
        cact = sb("cact", [P, KD])
        lb = sb("lb", [P, 3, 4])
        lbs = sb("lbs", [P, 4, 4])
        stat = sb("stat", [P, 4, NT])
        smal = sb("smal", [P, 2, 4, NCH])
        PS = ctx.enter_context(nc.psum_tensor("PS", [P, 8, 512], F32))

        def K(name):
            a, b = CONST_AT[name]
            return C[:, a:b]

        ident = K("ident")
        ones = K("ones")
        slot = [ring[:, s, :].rearrange("p (k n) -> p k n", k=8) for s in range(6)]
        slot_down = [ring[:, s, :].rearrange("p (k n) -> p k n", k=KE) for s in range(6)]

        at = [0]

        def sc(n):
            at[0] += n
            assert at[0] <= 2 * UNIT
            return SC[:, at[0] - n:at[0]]

        EB = [sc(512), sc(512)]
        BB = sc(512)
        KTS = sc(512).rearrange("p (i n) -> p i n", i=NT)
        SM = sc(512)
        SQ = sc(1024).rearrange("p (a n) -> p a n", a=2)
        RR = sc(512)
        shared = at[0]
        KB = [sc(512), sc(512)]
        SMR = sc(512)
        STH = sc(1024).rearrange("p (c n) -> p c n", c=8)
        SW = sc(512)
        ACC = [sc(512), sc(512)]
        at[0] = shared
        STG = sc(2048).rearrange("p (c n) -> p c n", c=8)
        at[0] = shared
        rows1 = sc(128)
        rows2 = sc(128)

        def mx(k, n=1):
            return MX[:, k * 512:(k + n) * 512]

        def four(k):
            return MX[:, k * 512:(k + 4) * 512].rearrange("p (h n) -> p h n", h=4)

        FH, QH, VH, QR, KR_, VR = four(0), four(4), four(8), four(12), four(16), four(20)
        QG, KG, LA = four(0), four(4), four(16)
        VG = MX[:, 8 * 512:16 * 512].rearrange("p (t n) -> p t n", t=NT)
        A2 = MX[0:GLA_RANK, 20 * 512:21 * 512]
        GA = MX[0:GLA_RANK, 21 * 512:22 * 512]
        WT = MX[:, 22 * 512:22 * 512 + KD * GLA_RANK].rearrange("p (k n) -> p k n", k=KD)
        GB = mx(0, 2)
        DG = mx(2)
        JUNK = mx(3, 2)
        FW = mx(13, 2)
        G = [mx(5, 2), mx(7, 2)]
        GT = [mx(9, 2).rearrange("p (k n) -> p k n", k=KD), mx(11, 2).rearrange("p (k n) -> p k n", k=KD)]
        SG = mx(13)
        AA = mx(14)
        AT = mx(15).rearrange("p (k n) -> p k n", k=KE)
        Y = [mx(16, 2), mx(18, 2)]
        YG = [[mx(5, 2), mx(7, 2)], [mx(9, 2), mx(11, 2)]]
        RT = MX[:, 20 * 512:24 * 512].rearrange("p (n i e) -> p n i e", n=32, i=NT)
        ZERO = mx(22, 2)
        CMF = mx(5)
        lists_rows = MX[0:NLIST, 23 * 512:23 * 512 + P]
        small = sb("small", [P, 12, NT])
        slots = sb("slots", [P, 2, NT], U32)
        rowt = sb("rowt", [P, 8, E])
        ctrlf = sb("ctrlf", [P, 1 + NLIST])
        ctrl = sb("ctrl", [P, 1 + NLIST], U32)
        lists = sb("lists", [P, NLIST], U32)
        cur = sb("cur", [P, 2], U32)

        xn_dram = [dram(f"xn_dram{l}", [S, D]) for l in range(DEPTH)]
        y_dram = dram("y_dram", [(E + MAXOVER) * P, D])
        list_dram = [dram(f"list_dram{l}", [NLIST * P, 1]) for l in range(DEPTH)]

        consts_in = sem("consts_in")
        x_in = sem("x_in")
        rows_in = sem("rows_in")
        cols_in = sem("cols_in")
        lists_zeroed = sem("lists_zeroed")
        zero_set = sem("zero_set")
        unit_in = [[sem(f"unit_in{l}_{s}") for s in range(4)] for l in range(DEPTH)]
        tail_in = sem("tail_in")
        fw_in = sem("fw_in")
        out_done = sem("out_done")
        dve_step = sem("dve_step")
        act_step = sem("act_step")
        rowsT = sem("rowsT")
        rows_copied = sem("rows_copied")
        c_ready = sem("c_ready")
        lbmax_ready = sem("lbmax_ready")
        lbexp_ready = sem("lbexp_ready")
        ada_acc = sem("ada_acc")
        ada_col = sem("ada_col")
        ada_stored = sem("ada_stored")
        squares = sem("squares")
        var_ready = sem("var_ready")
        std_ready = sem("std_ready")
        xn_ready = sem("xn_ready")
        hT_psum = sem("hT_psum")
        hT_act = sem("hT_act")
        hT_dve = sem("hT_dve")
        proj_done = sem("proj_done")
        gate_silu = sem("gate_silu")
        taken = [sem("taken0"), sem("taken1")]
        rotated = sem("rotated")
        fin_ready = sem("fin_ready")
        low_done = sem("low_done")
        low_copied = sem("low_copied")
        low_z = sem("low_z")
        low_biased = sem("low_biased")
        low_ln = sem("low_ln")
        f_ready = sem("f_ready")
        lnf_ready = sem("lnf_ready")
        mid_ready = sem("mid_ready")
        exp_ready = sem("exp_ready")
        qk_ready = sem("qk_ready")
        scores_done = sem("scores_done")
        keysT_done = sem("keysT_done")
        masked = sem("masked")
        keys_copied = sem("keys_copied")
        u_done = sem("u_done")
        states_ready = sem("states_ready")
        o_done = sem("o_done")
        o_squared = sem("o_squared")
        o_sum = sem("o_sum")
        o_rstd = sem("o_rstd")
        o_stored = sem("o_stored")
        diag_ready = sem("diag_ready")
        gb_psum = sem("gb_psum")
        gb_ready = sem("gb_ready")
        logits_done = sem("logits_done")
        logits_shifted = sem("logits_shifted")
        logits_exp = sem("logits_exp")
        picks_ready = sem("picks_ready")
        ranks_done = sem("ranks_done")
        slots_ready = sem("slots_ready")
        ctrl_ready = sem("ctrl_ready")
        xn_stored = sem("xn_stored")
        ids_scattered = sem("ids_scattered")
        lists_in = sem("lists_in")
        listsT = sem("listsT")
        lists_ready = sem("lists_ready")
        m = []
        for l in range(DEPTH):
            names = ("gateA upA downA gateB upB downB rows_gatheredA rows_gatheredB rowsT_done gt_act gt_dve "
                     "gate_done up_done silu_done prod_done prodT_done prodT_copied down_done y_ready y_storedA "
                     "y_storedB cur_set").split()
            m.append({n: sem(f"{n}{l}") for n in names})
        yg_in = [sem(f"yg_in{b}") for b in range(4)]
        combined = sem("combined")
        x_ready = sem("x_ready")

        block = ctx.enter_context(nc.Block())

        def unit_slot(layer, key):
            n = units[layer].index(key)
            return n % 4, 16 * (n // 4 + 1)

        def expert_rows(w, l, e, rows):
            flat = w.rearrange("l e r n -> (l e r) n")
            base = e * rows + l * E * rows
            return flat[bass.ds(base, rows), :].rearrange("(k p) n -> p k n", p=P)

        ADA_SRC = [w_ada[a // NADA, :, (a % NADA) * 512:(a % NADA) * 512 + 512].rearrange("(k p) n -> p k n", p=P)
                   for a in range(DEPTH * NADA)]

        def unit_source(layer, key):
            if key[0] == "ada":
                return ADA_SRC[key[1]]
            name = key[1]
            if name.startswith("wo"):
                w = (w_out_even if layer == 0 else w_out_odd)[0]
                col = int(name[2])
            else:
                w = (w_in_even if layer == 0 else w_in_odd)[0]
                col = W_COLS[name]
            return w[:, col * 512:col * 512 + 512].rearrange("(k p) n -> p k n", p=P)

        def used_after(layer, key):
            last = None
            for step, n in phases[layer]:
                if key[0] == "ada" and step == ("ada", key[1]):
                    last = (ada_acc, n + 1)
                if key[0] == "w" and step[0] == "proj" and step[1] == key[1]:
                    last = (proj_done, n + 1)
            return last

        LAST_CORE = [8, 12]
        EXPERT = [("gateA", w_gate, D, 0, 0), ("upA", w_up, D, 0, 1), ("downA", w_down, DE, 0, 2),
                  ("gateB", w_gate, D, 1, 3), ("upB", w_up, D, 1, 4), ("downB", w_down, DE, 1, 5)]

        @block.sync
        def _(sp):
            sp.dma_start(X[:, :, :], x[0].rearrange("(t p) d -> p t d", p=P)).then_inc(x_in, 16)
            regs = [sp.alloc_register(f"sp_r{k}") for k in range(9)]
            last_pair = None
            for l in range(DEPTH):
                for n, key in enumerate(units[l]):
                    if n == 4 and l == 1:
                            sp.wait_ge(x_ready, 2)
                            sp.dma_start(WT, w_in_odd[0, :, 6 * 512:6 * 512 + GLA_RANK].rearrange("(k p) n -> p k n", p=P)
                                         ).then_inc(tail_in, 16)
                            sp.dma_start(A2, w_gla_a2[0]).then_inc(tail_in, 16)
                    if n >= 4:
                        sp.wait_ge(*used_after(l, units[l][n - 4]))
                    elif l == 1:
                        s_, v = ((m[0]["gate_done"], last_pair * 2 + 1), (m[0]["up_done"], last_pair * 4 + 2),
                                 (m[0]["down_done"], last_pair * 2 + 1), (m[0]["gate_done"], last_pair * 2 + 2))[n]
                        v = keep(sp, regs[8], v)
                        sp.wait_ge(s_, v)
                    s, _v = unit_slot(l, key)
                    sp.dma_start(slot[s], unit_source(l, key)).then_inc(unit_in[l][s], 16)
                for name, w, rows, b, s in EXPERT:
                    if s < 4:
                        n = [k for k in range(len(units[l])) if k % 4 == s][-1]
                        sp.wait_ge(*used_after(l, units[l][n]))
                    else:
                        sp.wait_ge(o_stored, LAST_CORE[l])
                        sp.wait_ge(ada_stored, DEPTH * NADA)
                    view = slot_down[s] if rows == DE else slot[s]
                    sp.dma_start(view, expert_rows(w, l, b, rows)).then_inc(m[l][name], 16)
                sp.wait_ge(ctrl_ready, l + 1)
                last_pair = sp.value_load(ctrl[0:1, 0:1], min_val=E // 2 - 1, max_val=(E + MAXOVER) // 2 - 1)
                pairs = last_pair + 1
                with sp.Fori(0, last_pair) as i0:
                    for b in range(2):
                        expert = sp.value_load(ctrl[0:1, bass.ds(i0 * 2 + (3 + b), 1)], min_val=0, max_val=E - 1)
                        vals = [keep(sp, regs[3 * b], i0 * 2 + (b + 1)), keep(sp, regs[3 * b + 1], i0 * 4 + (2 * b + 2))]
                        for (name, w, rows, _, s), (done, v) in zip(
                                EXPERT[3 * b:3 * b + 3],
                                ((m[l]["gate_done"], vals[0]), (m[l]["up_done"], vals[1]), (m[l]["down_done"], vals[0]))):
                            src = expert_rows(w, l, expert, rows)
                            sp.wait_ge(done, v)
                            view = slot_down[s] if rows == DE else slot[s]
                            sp.dma_start(view, src).then_inc(m[l][name], 16)
            sp.wait_ge(x_ready, 4)
            sp.dma_start(FW, final_norm_w.rearrange("(o n) -> o n", o=1).to_broadcast([P, D])).then_inc(fw_in, 16)

        @block.gpsimd
        def _(pool):
            regs = [pool.alloc_register(f"pool_r{k}") for k in range(6)]
            nc.gpsimd.memset(ZERO, 0.0).then_inc(zero_set, 1)
            pool.wait_ge(zero_set, 1)
            for l in range(DEPTH):
                pool.dma_start(list_dram[l].rearrange("(c p) o -> c (p o)", p=P), lists_rows).then_inc(lists_zeroed, 16)
            for k in range(E, E + MAXOVER):
                pool.dma_start(y_dram[k * P:(k + 1) * P, :], ZERO).then_inc(lists_zeroed, 16)
            for l in range(DEPTH):
                ml = m[l]
                pool.wait_ge(lists_zeroed, 16 * (DEPTH + MAXOVER))
                pool.wait_ge(slots_ready, l + 1)
                tok = K("tokid")
                n = 0
                for i in range(NT):
                    for k in range(2):
                        pool.indirect_dma_start(list_dram[l], bass.IndirectOffsetOnAxis(ap=slots[:, k, i:i + 1], axis=0),
                                                tok[:, i:i + 1], None).then_inc(ids_scattered, 16)
                        n += 1
                pool.wait_ge(ids_scattered, 16 * 8 * (l + 1))
                pool.dma_start(lists_rows, list_dram[l].rearrange("(c p) o -> c (p o)", p=P)).then_inc(lists_in, 16)
                pool.wait_ge(ctrl_ready, l + 1)
                pairs = pool.value_load(ctrl[0:1, 0:1], min_val=E // 2 - 1, max_val=(E + MAXOVER) // 2 - 1) + 1
                pool.wait_ge(lists_ready, l + 1)
                pool.wait_ge(xn_stored, 16 * (l + 1))

                def gather(col, b, done_cur):
                    nc.gpsimd.tensor_copy(cur[:, b:b + 1], lists[:, col]).then_inc(ml["cur_set"], 1)
                    pool.wait_ge(lists_ready, l + 1)
                    pool.wait_ge(ml["cur_set"], done_cur)
                    pool.indirect_dma_start(G[b], None, xn_dram[l],
                                            bass.IndirectOffsetOnAxis(ap=cur[:, b:b + 1], axis=0)
                                            ).then_inc(ml["rows_gatheredA" if b == 0 else "rows_gatheredB"], 16)

                gather(slice(0, 1), 0, 1)
                gather(slice(1, 2), 1, 2)
                with pool.Fori(0, pairs) as i:
                    for b in range(2):
                        r_tr = keep(pool, regs[0], i * 4 + (2 * b + 2))
                        r_cur = keep(pool, regs[1], i * 2 + (b + 3))
                        r_y = keep(pool, regs[2], i * 4 + (2 * b + 2))
                        r_row = keep(pool, regs[3], i * (2 * P) + b * P)
                        r_col = keep(pool, regs[4], i * 2 + (b + 2))
                        pool.wait_ge(lists_ready, l + 1)
                        pool.wait_ge(ml["rowsT_done"], r_tr)
                        gather(bass.ds(r_col, 1), b, r_cur)
                        pool.wait_ge(lists_ready, l + 1)
                        pool.wait_ge(ml["y_ready"], r_y)
                        pool.dma_start(y_dram[bass.ds(r_row, P), :], Y[b]
                                       ).then_inc(ml["y_storedA" if b == 0 else "y_storedB"], 16)
                last = keep(pool, regs[5], pairs * 16)
                more = keep(pool, regs[0], pairs * 16 + 16)
                more4 = keep(pool, regs[1], pairs * 4 + 2)
                pool.wait_ge(slots_ready, l + 1)
                pool.wait_ge(ml["y_storedA"], last)
                pool.wait_ge(ml["y_storedB"], last)
                pool.wait_ge(ml["rows_gatheredA"], more)
                pool.wait_ge(ml["rows_gatheredB"], more)
                pool.wait_ge(ml["rowsT_done"], more4)
                for i in range(NT):
                    if i >= 2:
                        pool.wait_ge(combined, NT * l + i - 1)
                    for k in range(2):
                        pool.indirect_dma_start(YG[i % 2][k], None, y_dram,
                                                bass.IndirectOffsetOnAxis(ap=slots[:, k, i:i + 1], axis=0)
                                                ).then_inc(yg_in[2 * (i % 2) + k], 16)

        @block.scalar
        def _(act):
            me = Chain(act, act_step)
            a = nc.scalar.activation
            act.dma_start(C[:, :], consts).then_inc(consts_in, 16)
            act.dma_start(CMF, cmask).then_inc(consts_in, 16)
            rv = lambda t, w: t.rearrange("a (r w) -> (a r) w", w=w)
            act.dma_start(rows1[0:96, :], rv(b_ada, P)).then_inc(rows_in, 16)
            act.dma_start(rows1[96:112, :], rv(norm_mix_w, P)).then_inc(rows_in, 16)
            act.dma_start(rows1[112:128, :], rv(norm_ffn_w, P)).then_inc(rows_in, 16)
            at_ = 0
            for t in (c, hg_lb_logits, hg_norm_w, ret_norm_w, b_gla_a2, gla_norm_w):
                r = t.shape[0] * t.shape[1] // P
                act.dma_start(rows2[at_:at_ + r, :], rv(t, P)).then_inc(rows_in, 16)
                at_ += r
            act.dma_start(WR[:, :, :], w_router.rearrange("(k p) n -> p k n", p=P)).then_inc(cols_in, 16)
            act.dma_start(BR[:, :], b_router.rearrange("(o n) -> o n", o=1).to_broadcast([P, E])).then_inc(cols_in, 16)
            act.wait_ge(rows_copied, 1)
            a(cact[:, :], VC[:, 128:136], ACT.Silu).then_inc(c_ready, 1)
            act.wait_ge(lbmax_ready, 1)
            a(lb[:, :, :], lb[:, :, :], ACT.Exp).then_inc(lbexp_ready, 1)

            def norm(n):
                if n == 0:
                    act.wait_ge(x_in, 16)
                else:
                    act.wait_ge(x_ready, n)
                for i in range(NT):
                    me.link(a(JUNK, X[:, i, :], ACT.Square, accum_out=stat[:, 0, i:i + 1]))
                a(stat[:, 0, :], stat[:, 0, :], ACT.Copy).then_inc(squares, 1)
                act.wait_ge(var_ready, n + 1)
                a(stat[:, 2, :], stat[:, 1, :], ACT.Sqrt).then_inc(std_ready, 1)

            def to_hT(n, n_ht):
                shift = (n // 2) * 48 + (n % 2) * 24
                for k in range(0, KD, 2):
                    act.wait_ge(hT_psum, KD * n_ht + k + 1)
                    a(HT[:, k, :], PS[:, k % 2, :], ACT.Identity, bias=MOD[:, shift + k:shift + k + 1],
                      scale=AM[:, n, k:k + 1]).then_inc(hT_act, 1)

            def gate_rows(n):
                for half in range(2):
                    act.wait_ge(gb_psum, 2 * n + half + 1)
                    a(GB[:, half * 512:half * 512 + 512], PS[:, 7, :], ACT.Copy).then_inc(gb_ready, 1)

            for l in range(DEPTH):
                for (kind, *arg), n in phases[l]:
                    if kind == "norm":
                        norm(arg[0])
                        to_hT(arg[0], arg[0])
                    elif kind == "low":
                        act.wait_ge(low_done, 1)
                        a(GA, PS[0:GLA_RANK, 7, :], ACT.Copy).then_inc(low_copied, 1)
                        for h in range(HEADS):
                            act.wait_ge(low_biased, h + 1)
                            me.link(a(EB[0], EB[0], ACT.Abs))
                            me.link(a(EB[0], EB[0], ACT.Exp, scale=-1.0))
                            a(EB[0], EB[0], ACT.Ln, bias=1.0).then_inc(low_ln, 1)
                    elif kind == "proj":
                        name, g = arg
                        bank = PS[:, n % 2, :]
                        if name in ("rq", "rk"):
                            dst = QR if name == "rq" else KR_
                            ri = rot_index(name, g)
                            act.wait_ge(proj_done, n + 1)
                            if ri:
                                act.wait_ge(rotated, ri)
                            me.add(a(dst[:, g, :], bank, ACT.Copy))
                            me.add(a(SW[64:128, :], bank[0:64, :], ACT.Copy))
                            a(SW[0:64, :], bank[64:128, :], ACT.Copy).then_inc(taken[n % 2], 1)
                        elif name in ("hf", "hq"):
                            act.wait_ge(proj_done, n + 1)
                            a((FH if name == "hf" else QH)[:, g, :], bank, ACT.Sigmoid).then_inc(taken[n % 2], 1)
                        elif name in GATES:
                            act.wait_ge(proj_done, n + 1)
                            a(bank, bank, ACT.Silu).then_inc(gate_silu, 1)
                        elif name in ("gq", "gk"):
                            act.wait_ge(proj_done, n + 1)
                            a((QG if name == "gq" else KG)[:, g, :], bank, ACT.Copy).then_inc(taken[n % 2], 1)
                    elif kind == "prep":
                        what, h = arg
                        b = n % 2
                        if what == "ret":
                            continue
                        if what == "hg":
                            act.wait_ge(f_ready, h + 1)
                            a(FH[:, h, :], FH[:, h, :], ACT.Ln).then_inc(lnf_ready, 1)
                        F = FH if what == "hg" else LA
                        act.wait_ge(mid_ready, n - HEADS + 1)
                        act.wait_ge(o_done, n - 1)
                        me.add(a(EB[b], F[:, h, :], ACT.Exp))
                        for r in (1, 2, 3):
                            me.add(a(smal[:, b, r, :], smal[:, b, 0 if r == 1 else r, :], ACT.Exp))
                        me.wait()
                        a(F[:, h, :], F[:, h, :], ACT.Exp, scale=-1.0).then_inc(exp_ready, 1)
                    elif kind == "A":
                        what, h = arg
                        act.wait_ge(keysT_done, n + 1)
                        ps = PS[:, 3, :].rearrange("p (i n) -> p i n", i=NT)
                        if what == "ret":
                            a(KTS, ps, ACT.Copy, scale=K("kdecay")[:, h:h + 1]).then_inc(keys_copied, 1)
                        else:
                            a(KTS, ps, ACT.Copy).then_inc(keys_copied, 1)
                    elif kind == "C":
                        what, h = arg
                        nh = 2 if what == "gla" else 1
                        act.wait_ge(o_done, n + 1)
                        for d in range(nh):
                            a(SQ[:, d, :], PS[:, 6 + d, :], ACT.Square).then_inc(o_squared, 1)
                    elif kind == "D":
                        what, h = arg
                        dv = 256 if what == "gla" else 128
                        act.wait_ge(o_sum, n + 1)
                        me.link(a(RR, PS[:, 2, :], ACT.Ln, bias=K("eps"), scale=1.0 / dv))
                        a(RR, RR, ACT.Exp, scale=-0.5).then_inc(o_rstd, 1)
                    elif kind == "gb":
                        gate_rows(arg[0])
                n_ = 2 * l + 1
                ml = m[l]
                norm(n_)
                act.wait_ge(xn_ready, n_ + 1)
                act.dma_start(xn_dram[l].rearrange("(t p) d -> p t d", p=P), XN).then_inc(xn_stored, 16)
                to_hT(n_, n_)
                act.wait_ge(logits_shifted, l + 1)
                a(RT[:, 0, :, :], RT[:, 0, :, :], ACT.Exp).then_inc(logits_exp, 1)
                gate_rows(n_)
                regs = [act.alloc_register(f"act{l}_r{k}") for k in range(4)]
                act.wait_ge(ctrl_ready, l + 1)
                pairs = act.value_load(ctrl[0:1, 0:1], min_val=E // 2 - 1, max_val=(E + MAXOVER) // 2 - 1) + 1
                shift = l * 48 + 24

                def rows_out(b, v):
                    act.wait_ge(ml["rowsT_done"], v)
                    for k in range(4):
                        ins = a(GT[b][:, k, :], PS[:, 0, k * P:(k + 1) * P], ACT.Identity,
                                bias=MOD[:, shift + k:shift + k + 1], scale=AM[:, n_, k:k + 1])
                    ins.then_inc(ml["gt_act"], 1)

                rows_out(0, 1)
                with act.Fori(0, pairs) as i:
                    i2 = keep(act, regs[0], i * 2)
                    i4 = keep(act, regs[1], i * 4)
                    for b in range(2):
                        act.wait_ge(ml["gate_done"], i2 + (b + 1))
                        act.wait_ge(ml["prod_done"], i4 + 2 * b)
                        a(SG, PS[:, 2, :], ACT.Silu).then_inc(ml["silu_done"], 1)
                        rows_out(1 - b, i4 + (2 * b + 3))
                        for f in range(2):
                            act.wait_ge(ml["prodT_done"], i4 + (2 * b + f + 1))
                            a(AT[:, 2 * f:2 * f + 2, :],
                              PS[:, 5, f * 256:(f + 1) * 256].rearrange("p (k n) -> p k n", k=2),
                              ACT.Copy).then_inc(ml["prodT_copied"], 1)
            norm(4)
            for i in range(NT):
                act.wait_ge(fin_ready, i + 1)
                act.dma_start(out[0, i * P:(i + 1) * P, :], XN[:, i, :]).then_inc(out_done, 16)
            act.wait_ge(out_done, 16 * NT)

        def took(layer, name, g):
            n = next(k for step, k in phases[layer] if step == ("proj", name, g))
            return taken[n % 2], n // 2 + 1

        @block.vector
        def _(dve):
            me = Chain(dve, dve_step)
            v = nc.vector
            tt, ts, stt = v.tensor_tensor, v.tensor_scalar, v.scalar_tensor_tensor
            dve.wait_ge(rowsT, 1)
            v.tensor_copy(VC[:, :], PS[:, 0, 0:168]).then_inc(rows_copied, 1)
            dve.wait_ge(rows_copied, 1)
            L = VC[:, 136:148].rearrange("p (r h) -> p r h", r=3)
            me.link(tt(lbs[:, 0, :], L[:, 0, :], L[:, 1, :], ALU.max))
            me.link(tt(lbs[:, 1, :], lbs[:, 0, :], L[:, 2, :], ALU.max))
            tt(lb[:, :, :], L, lbs[:, 1:2, :].to_broadcast([P, 3, 4]), ALU.subtract).then_inc(lbmax_ready, 1)
            dve.wait_ge(lbexp_ready, 1)
            me.link(tt(lbs[:, 2, :], lb[:, 0, :], lb[:, 1, :], ALU.add))
            me.link(tt(lbs[:, 3, :], lbs[:, 2, :], lb[:, 2, :], ALU.add))
            me.link(v.reciprocal(lbs[:, 2, :], lbs[:, 3, :]))
            me.link(tt(lbs[:, 0, :], lb[:, 0, :], lbs[:, 2, :], ALU.mult))
            me.link(ts(lbs[:, 1, :], lbs[:, 0, :], -1.0, 1.0, ALU.mult, ALU.add))
            dve.wait_ge(c_ready, 1)
            dve.wait_ge(consts_in, 32)
            me.link(v.tensor_copy(CM[:, :], CMF))

            n_core = 0

            def norm(n):
                dve.wait_ge(squares, n + 1)
                ts(stat[:, 1, :], stat[:, 0, :], 1.0 / D, EPS, ALU.mult, ALU.add).then_inc(var_ready, 1)
                dve.wait_ge(std_ready, n + 1)
                me.link(v.reciprocal(stat[:, 3, :], stat[:, 2, :]))
                if n >= 2:
                    dve.wait_ge(xn_stored, 16 * (n // 2))
                if n == 4:
                    dve.wait_ge(fw_in, 16)
                    for i in range(NT):
                        stt(XN[:, i, :], X[:, i, :], stat[:, 3, i:i + 1], FW, ALU.mult, ALU.mult).then_inc(fin_ready, 1)
                    return
                base = (n // 2) * 48 + (n % 2) * 24
                w = VC[:, 96 + 16 * (n % 2) + KD * (n // 2):][:, 0:KD]
                me.add(stt(AM[:, n, :], MOD[:, base + KD:base + 2 * KD], 1.0, w, ALU.add, ALU.mult))
                for i in range(NT):
                    ins = ts(XN[:, i, :], X[:, i, :], stat[:, 3, i:i + 1], None, ALU.mult)
                    if i < NT - 1:
                        me.add(ins)
                ins.then_inc(xn_ready, 1)
                me.wait()
                for k in range(1, KD, 2):
                    dve.wait_ge(hT_psum, KD * n + k + 1)
                    ts(HT[:, k, :], PS[:, k % 2, :], AM[:, n, k:k + 1], MOD[:, base + k:base + k + 1],
                       ALU.mult, ALU.add).then_inc(hT_dve, 1)

            def gate_diagonals(n):
                gate = (n // 2) * 48 + (n % 2) * 24 + 16
                for half in range(2):
                    if n or half:
                        dve.wait_ge(gb_psum, 2 * n + half)
                    for j in range(4):
                        ins = ts(DG[:, j * P:(j + 1) * P], ident, MOD[:, gate + 4 * half + j:gate + 4 * half + j + 1],
                                 None, ALU.mult)
                        if j < 3:
                            me.add(ins)
                    ins.then_inc(diag_ready, 1)

            def decays(F, K_, Q, h, b, qscale):
                me.link(v.tensor_tensor_scan(BB, K("scanmask"), F[:, h, :], 0.0, ALU.mult, ALU.add))
                B3 = BB.rearrange("p (c n) -> p c n", c=NCH)
                mid = B3[:, :, CHUNK // 2 - 1:CHUNK // 2]
                me.add(v.tensor_copy(smal[:, b, 0, :].unsqueeze(2), mid))
                me.link(v.tensor_copy(smal[:, b, 3, :].unsqueeze(2), B3[:, :, CHUNK - 1:CHUNK]))
                me.add(tt(smal[:, b, 2, :], smal[:, b, 3, :], smal[:, b, 0, :], ALU.subtract))
                tt(F[:, h, :].rearrange("p (c n) -> p c n", c=NCH), B3, mid.to_broadcast([P, NCH, CHUNK]),
                   ALU.subtract).then_inc(mid_ready, 1)

            def decayed(F, K_, Q, b, qscale):
                c3 = lambda t: t.rearrange("p (c n) -> p c n", c=NCH)
                me.add(stt(Q, Q, qscale, EB[b], ALU.mult, ALU.mult))
                me.link(tt(K_, K_, F, ALU.mult))
                me.add(tt(c3(EB[b]), c3(Q), smal[:, b, 1, :].unsqueeze(2).to_broadcast([P, NCH, CHUNK]), ALU.mult))
                tt(c3(F), c3(K_), smal[:, b, 2, :].unsqueeze(2).to_broadcast([P, NCH, CHUNK]),
                   ALU.mult).then_inc(qk_ready, 1)
                me.wait()

            gates_seen = 0
            for l in range(DEPTH):
                me.link(v.memset(SM, 0.0))
                for (kind, *arg), n in phases[l]:
                    if kind == "norm":
                        norm(arg[0])
                    elif kind == "ada":
                        a_ = arg[0]
                        s, val = unit_slot(l, ("ada", a_))
                        dve.wait_ge(unit_in[l][s], val)
                        for k in range(KD):
                            if k == 0:
                                ins = ts(ACC[a_ % 2], slot[s][:, 0, :], cact[:, 0:1], None, ALU.mult)
                            else:
                                ins = stt(ACC[a_ % 2], slot[s][:, k, :], cact[:, k:k + 1], ACC[a_ % 2], ALU.mult, ALU.add)
                            if k < KD - 1:
                                me.link(ins)
                        ins.then_inc(ada_acc, 1)
                    elif kind == "adacol":
                        a_ = arg[0]
                        dve.wait_ge(ada_col, n + 1)
                        tt(MOD[:, 4 * a_:4 * a_ + 4], PS[:, 7, 0:4], VC[:, 4 * a_:4 * a_ + 4], ALU.add
                           ).then_inc(ada_stored, 1)
                        dve.wait_ge(ada_stored, n + 1)
                    elif kind == "low":
                        for h in range(HEADS):
                            z = PS[:, 4 + h % 2, :]
                            bias = VC[:, 156 + h:157 + h]
                            dve.wait_ge(low_z, h + 1)
                            me.add(ts(LA[:, h, :], z, bias, 0.0, ALU.add, ALU.min))
                            ts(EB[0], z, bias, None, ALU.add).then_inc(low_biased, 1)
                            dve.wait_ge(low_ln, h + 1)
                            me.link(tt(LA[:, h, :], LA[:, h, :], EB[0], ALU.subtract))
                            me.link(ts(LA[:, h, :], LA[:, h, :], 1.0 / 16.0, None, ALU.mult))
                    elif kind == "proj":
                        name, g = arg
                        bank = PS[:, n % 2, :]
                        if name in ("rq", "rk"):
                            Q = (QR if name == "rq" else KR_)[:, g, :]
                            dve.wait_ge(taken[n % 2], n // 2 + 1)
                            me.add(tt(Q, Q, K("cos"), ALU.mult))
                            me.link(tt(SW, SW, K("sin"), ALU.mult))
                            tt(Q, Q, SW, ALU.add).then_inc(rotated, 1)
                        elif name in ("rv", "hi", "gv0", "gv1"):
                            dst = {"rv": VR[:, g, :], "hi": VH[:, g, :], "gv0": VG[:, g, 0:512], "gv1": VG[:, g, 512:1024]}
                            dve.wait_ge(proj_done, n + 1)
                            dve.wait_ge(lists_zeroed, 16 * (DEPTH + MAXOVER))
                            v.tensor_copy(dst[name], bank).then_inc(taken[n % 2], 1)
                        elif name in GATES:
                            k = GATES[name] + g
                            w = {"hg": 148 + g, "rg": 152 + g, "gg0": 160 + g, "gg1": 164 + g}[name]
                            gates_seen += 1
                            dve.wait_ge(gate_silu, gates_seen)
                            dve.wait_ge(o_stored, n_core)
                            stt(OT[:, k, :], OT[:, k, :], VC[:, w:w + 1], bank, ALU.mult, ALU.mult
                                ).then_inc(taken[n % 2], 1)
                        elif name in ("wo0", "wo1"):
                            u = int(name[2])
                            dve.wait_ge(proj_done, n + 1)
                            dve.wait_ge(gb_ready, 4 * l + 2)
                            tt(JUNK[:, 0:512], bank, GB[:, u * 512:u * 512 + 512], ALU.mult).then_inc(taken[n % 2], 1)
                            dve.wait_ge(taken[n % 2], n // 2 + 1)
                            xs = X[:, g, u * 512:u * 512 + 512]
                            ins = tt(xs, xs, JUNK[:, 0:512], ALU.add)
                            if (u, g) == (1, 3):
                                ins.then_inc(x_ready, 1)
                            else:
                                me.link(ins)
                    elif kind == "prep":
                        what, h = arg
                        b = n % 2
                        if n >= 2:
                            dve.wait_ge(o_done, n - 1)
                        if what == "ret":
                            dve.wait_ge(rotated, rot_index("rk", h) + 1)
                            gr = K("gamrow")[:, h * P:(h + 1) * P].unsqueeze(1).to_broadcast([P, NT, P])
                            tt(EB[b].rearrange("p (i n) -> p i n", i=NT), QR[:, h, :].rearrange("p (i n) -> p i n", i=NT),
                               gr, ALU.mult).then_inc(qk_ready, 1)
                        elif what == "hg":
                            F = FH[:, h, :]
                            dve.wait_ge(*took(0, "hf", h))
                            dve.wait_ge(*took(0, "hq", h))
                            me.link(ts(F, F, lbs[:, 1, h:h + 1], lbs[:, 0, h:h + 1], ALU.mult, ALU.add))
                            ts(KB[b], F, -1.0, 1.0, ALU.mult, ALU.add).then_inc(f_ready, 1)
                            dve.wait_ge(lnf_ready, h + 1)
                            decays(FH, KB[b], None, h, b, 1.0)
                            dve.wait_ge(exp_ready, n - HEADS + 1)
                            decayed(F, KB[b], QH[:, h, :], b, 1.0)
                        else:
                            dve.wait_ge(*took(1, "gq", h))
                            dve.wait_ge(*took(1, "gk", h))
                            decays(LA, None, None, h, b, 1.0)
                            dve.wait_ge(exp_ready, n - HEADS + 1)
                            decayed(LA[:, h, :], KG[:, h, :], QG[:, h, :], b, float(P) ** -0.5)
                    elif kind == "A":
                        what, h = arg
                        dve.wait_ge(scores_done, n + 1)
                        if what == "ret":
                            i3 = lambda t: t.rearrange("p (i n) -> p i n", i=NT)
                            dec = K("decay")[:, h * P:(h + 1) * P].unsqueeze(1).to_broadcast([P, NT, P])
                            tt(i3(SMR), i3(PS[:, 2, :]), dec, ALU.mult).then_inc(masked, 1)
                        else:
                            v.copy_predicated(SM, CM[:, :], PS[:, 2, :]).then_inc(masked, 1)
                    elif kind == "B":
                        what, h = arg
                        b = n % 2
                        fills = FILLS[what]
                        ST = STG if what == "gla" else STH
                        width = 256 if what == "gla" else 128
                        fb = fills_before(n)
                        for f, cs in enumerate(fills):
                            dve.wait_ge(u_done, fb + f + 1)
                            for j, c_ in enumerate(cs):
                                bank_, col = update_at(what, c_)
                                u_ = PS[:, bank_, col:col + width]
                                if c_ == 0:
                                    ins = v.tensor_copy(ST[:, 1, :], u_)
                                else:
                                    dec = float(gamma[h]) if what == "ret" else smal[:, b, 3, c_:c_ + 1]
                                    ins = stt(ST[:, c_ + 1, :], ST[:, c_, :], dec, u_, ALU.mult, ALU.add)
                                if j < len(cs) - 1:
                                    me.link(ins)
                            ins.then_inc(states_ready, 1)
                            dve.wait_ge(states_ready, fb + f + 1)
                    elif kind == "D":
                        what, h = arg
                        dve.wait_ge(o_rstd, n + 1)
                        nh = 2 if what == "gla" else 1
                        for d in range(nh):
                            k = {"ret": 4 + h, "hg": h, "gla": 2 * h + d}[what]
                            ins = tt(OT[:, k, :], PS[:, 6 + d, :], RR, ALU.mult)
                            if d < nh - 1:
                                me.add(ins)
                        ins.then_inc(o_stored, 1)
                        n_core = n + 1
                    elif kind == "gb":
                        gate_diagonals(arg[0])
                n_ = 2 * l + 1
                ml = m[l]
                norm(n_)
                t = lambda k: RT[:, k, :, :]
                bc = lambda s_: s_.unsqueeze(2).to_broadcast([P, NT, E])
                LG, PR, SEL, TMP, OH1, OH2, SLE, MM, RK = (t(k) for k in range(9))
                red = lambda o, i_, op: v.tensor_reduce(o, i_, AX, op)
                sm_ = lambda k: small[:, k, :]
                dve.wait_ge(logits_done, l + 1)
                dve.wait_ge(cols_in, 32)
                lg = PS[:, 2, 0:NT * E].rearrange("p (i e) -> p i e", i=NT)
                me.link(red(sm_(0), lg, ALU.max))
                tt(LG, lg, bc(sm_(0)), ALU.subtract).then_inc(logits_shifted, 1)
                dve.wait_ge(logits_exp, l + 1)
                me.link(red(sm_(0), LG, ALU.add))
                me.link(v.reciprocal(sm_(1), sm_(0)))
                me.link(tt(PR, LG, bc(sm_(1)), ALU.mult))
                me.link(tt(SEL, PR, BR[:, :].unsqueeze(1).to_broadcast([P, NT, E]), ALU.add))
                g16 = lambda ap: ap.rearrange("p i (g e) -> p (i g) e", g=GROUPS)
                GSC = RT[:, 9, 0, :]
                GEQ = RT[:, 9, 1, :]
                GPN = RT[:, 9, 2, :]
                gi = lambda ap: ap.rearrange("p (i g) -> p i g", i=NT)
                me.link(red(GSC, g16(SEL), ALU.max))
                me.link(red(sm_(2), gi(GSC), ALU.max))
                bg = lambda s_: s_.unsqueeze(2).to_broadcast([P, NT, GROUPS])
                me.link(tt(gi(GEQ), gi(GSC), bg(sm_(2)), ALU.is_ge))
                me.link(stt(gi(GEQ), gi(GEQ), -BIG, K("iota_g_big").unsqueeze(1).to_broadcast([P, NT, GROUPS]),
                            ALU.mult, ALU.add))
                me.link(red(sm_(3), gi(GEQ), ALU.min))
                me.link(tt(gi(GSC), gi(GEQ), bg(sm_(3)), ALU.is_equal))
                me.link(ts(GPN, GSC, -1.0, 1e30, ALU.add, ALU.mult))
                b16 = lambda ap: ap.unsqueeze(2).to_broadcast([P, NT * GROUPS, EPG])
                me.link(tt(g16(SEL), g16(SEL), b16(GSC), ALU.mult))
                me.link(tt(g16(SEL), g16(SEL), b16(GPN), ALU.add))

                def pick(OH, s_):
                    me.link(red(sm_(s_), SEL, ALU.max))
                    me.link(tt(TMP, SEL, bc(sm_(s_)), ALU.is_ge))
                    me.link(stt(TMP, TMP, -BIG, K("iota_e_big").unsqueeze(1).to_broadcast([P, NT, E]), ALU.mult, ALU.add))
                    me.link(red(sm_(s_), TMP, ALU.min))
                    me.link(tt(OH, TMP, bc(sm_(s_)), ALU.is_equal))

                pick(OH1, 4)
                me.link(stt(SEL, OH1, -3e38, SEL, ALU.mult, ALU.add))
                pick(OH2, 5)
                tt(MM, OH1, OH2, ALU.add).then_inc(picks_ready, 1)
                for OH, o_ in ((OH1, 6), (OH2, 7)):
                    me.link(tt(TMP, PR, OH, ALU.mult))
                    me.link(red(sm_(o_), TMP, ALU.add))
                me.link(tt(sm_(8), sm_(6), sm_(7), ALU.add))
                me.link(v.reciprocal(sm_(9), sm_(8)))
                me.add(tt(sm_(6), sm_(6), sm_(9), ALU.mult))
                me.add(tt(sm_(7), sm_(7), sm_(9), ALU.mult))
                dve.wait_ge(ranks_done, l + 1)
                me.add(v.tensor_copy(RK, PS[:, 3, 0:NT * E].rearrange("p (i e) -> p i e", i=NT)))
                me.link(v.tensor_copy(rowt[:, 0, :], PS[:, 3, NT * E:NT * E + E]))
                me.link(ts(rowt[:, 1, :], rowt[:, 0, :], float(P), None, ALU.is_gt))
                me.link(stt(rowt[:, 1, :], rowt[:, 0, :], float(2 * P), rowt[:, 1, :], ALU.is_gt, ALU.add))
                me.link(stt(rowt[:, 1, :], rowt[:, 0, :], float(3 * P), rowt[:, 1, :], ALU.is_gt, ALU.add))
                me.link(v.tensor_tensor_scan(rowt[:, 2, :], ones[:, 0:E], rowt[:, 1, :], 0.0, ALU.mult, ALU.add))
                me.link(tt(rowt[:, 3, :], rowt[:, 2, :], rowt[:, 1, :], ALU.subtract))
                me.link(tt(rowt[:, 3, :], rowt[:, 3, :], K("iota_e"), ALU.subtract))
                me.link(ts(rowt[:, 3, :], rowt[:, 3, :], float(E - 1), float(P), ALU.add, ALU.mult))
                me.link(ts(TMP, RK, float(P), None, ALU.is_ge))
                me.link(tt(TMP, TMP, rowt[:, 3:4, :].to_broadcast([P, NT, E]), ALU.mult))
                me.link(tt(SLE, TMP, RK, ALU.add))
                me.link(stt(SLE, K("iota_e").unsqueeze(1).to_broadcast([P, NT, E]), float(P), SLE, ALU.mult, ALU.add))
                for OH, k in ((OH1, 0), (OH2, 1)):
                    me.link(tt(TMP, SLE, OH, ALU.mult))
                    me.link(red(sm_(10 + k), TMP, ALU.add))
                me.add(v.tensor_copy(slots[:, 0, :], sm_(10)))
                v.tensor_copy(slots[:, 1, :], sm_(11)).then_inc(slots_ready, 1)
                me.link(v.memset(ctrlf[:, :], 0.0))
                me.link(v.tensor_copy(ctrlf[:, 1:1 + E], K("iota_e")))
                cmp8 = RT[:, 10:12, :, :].rearrange("p a i e -> p (a i) e")
                me.link(tt(cmp8, rowt[:, 2:3, :].to_broadcast([P, MAXOVER, E]),
                           K("iota_j").unsqueeze(2).to_broadcast([P, MAXOVER, E]), ALU.is_le))
                me.link(red(ctrlf[:, 1 + E:1 + E + MAXOVER], cmp8, ALU.add))
                me.link(ts(ctrlf[:, 1 + E:1 + E + MAXOVER], ctrlf[:, 1 + E:1 + E + MAXOVER], float(E - 1), None, ALU.min))
                total = rowt[:, 2, E - 1:E]
                me.link(ts(ctrlf[:, 0:1], total, 0.0, float(E // 2 - 1), ALU.is_gt, ALU.add))
                for k in range(2, MAXOVER, 2):
                    me.link(stt(ctrlf[:, 0:1], total, float(k), ctrlf[:, 0:1], ALU.is_gt, ALU.add))
                v.tensor_copy(ctrl[:, :], ctrlf[:, :]).then_inc(ctrl_ready, 1)
                gate_diagonals(n_)
                dve.wait_ge(listsT, l + 1)
                v.tensor_copy(lists[:, :], PS[:, 3, 0:NLIST]).then_inc(lists_ready, 1)
                dve.wait_ge(ctrl_ready, l + 1)
                pairs = dve.value_load(ctrl[0:1, 0:1], min_val=E // 2 - 1, max_val=(E + MAXOVER) // 2 - 1) + 1
                regs = [dve.alloc_register(f"dve{l}_r{k}") for k in range(4)]
                shift = l * 48 + 24

                def rows_out(b, val):
                    dve.wait_ge(ml["rowsT_done"], val)
                    for k in range(4, KD):
                        ins = ts(GT[b][:, k, :], PS[:, 1, (k - 4) * P:(k - 3) * P], AM[:, n_, k:k + 1],
                                 MOD[:, shift + k:shift + k + 1], ALU.mult, ALU.add)
                    ins.then_inc(ml["gt_dve"], 1)

                rows_out(0, 2)
                dve.wait_ge(gb_ready, 2 * n_ + 2)
                with dve.Fori(0, pairs) as i:
                    i2 = keep(dve, regs[0], i * 2)
                    i4 = keep(dve, regs[1], i * 4)
                    i16 = keep(dve, regs[2], i * 16)
                    for b in range(2):
                        rows_out(1 - b, i4 + (2 * b + 4))
                        for f in range(2):
                            dve.wait_ge(ml["silu_done"], i2 + (b + 1))
                            dve.wait_ge(ml["up_done"], i4 + (2 * b + f + 1))
                            tt(AA[:, f * 256:(f + 1) * 256], SG[:, f * 256:(f + 1) * 256], PS[:, 3 + f, 0:256],
                               ALU.mult).then_inc(ml["prod_done"], 1)
                        dve.wait_ge(ml["down_done"], i2 + (b + 1))
                        dve.wait_ge(ml["y_storedA" if b == 0 else "y_storedB"], i16)
                        for h_ in range(2):
                            tt(Y[b][:, h_ * 512:h_ * 512 + 512], PS[:, 6 + h_, :], GB[:, h_ * 512:h_ * 512 + 512],
                               ALU.mult).then_inc(ml["y_ready"], 1)
                for i in range(NT):
                    for k in range(2):
                        q = 2 * (i % 2) + k
                        dve.wait_ge(yg_in[q], 16 * (2 * l + i // 2 + 1))
                        ins = stt(X[:, i, :], YG[i % 2][k], sm_(6 + k)[:, i:i + 1], X[:, i, :], ALU.mult, ALU.add)
                        if k == 0:
                            me.link(ins)
                        elif i < NT - 1:
                            ins.then_inc(combined, 1)
                        else:
                            ins.then_inc(x_ready, 1)
            norm(4)

        @block.tensor
        def _(pe):
            mm = nc.tensor.matmul
            pe.wait_ge(consts_in, 32)
            pe.wait_ge(rows_in, 16 * 9)
            nc.tensor.transpose(PS[:, 0, 0:128], rows1, ident)
            nc.tensor.transpose(PS[:, 0, 128:168], rows2[0:40, :], ident[0:40, 0:40]).then_inc(rowsT, 1)
            pe.wait_ge(rows_copied, 1)

            def to_hT(n):
                pe.wait_ge(xn_ready, n + 1)
                for k in range(KD):
                    if k >= 2:
                        pe.wait_ge(hT_act if k % 2 == 0 else hT_dve, 4 * n + k // 2)
                    for i in range(NT):
                        ins = nc.tensor.transpose(PS[:, k % 2, i * P:(i + 1) * P], XN[:, i, k * P:(k + 1) * P], ident)
                    ins.then_inc(hT_psum, 1)

            def hT_complete(n):
                pe.wait_ge(hT_act, 4 * n + 4)
                pe.wait_ge(hT_dve, 4 * n + 4)

            def gate_rows(n):
                for half in range(2):
                    pe.wait_ge(diag_ready, 2 * n + half + 1)
                    if n or half:
                        pe.wait_ge(gb_ready, 2 * n + half)
                    mm(PS[:, 7, :], ones, DG, start=True, stop=True).then_inc(gb_psum, 1)

            rows_made = 0
            for l in range(DEPTH):
                for (kind, *arg), n in phases[l]:
                    if kind == "norm":
                        to_hT(arg[0])
                        hT_complete(arg[0])
                    elif kind == "adacol":
                        a_ = arg[0]
                        pe.wait_ge(ada_acc, a_ + 1)
                        pe.wait_ge(ada_stored, n)
                        if rows_made:
                            pe.wait_ge(gb_ready, rows_made)
                        for j in range(4):
                            ins = mm(PS[:, 7, j:j + 1], ACC[a_ % 2][:, j * P:(j + 1) * P], ones[:, 0:1], start=True, stop=True)
                        ins.then_inc(ada_col, 1)
                    elif kind == "low":
                        pe.wait_ge(tail_in, 32)
                        for k in range(KD):
                            ins = mm(PS[0:GLA_RANK, 7, :], WT[:, k, :], HT[:, k, :], start=k == 0, stop=k == KD - 1)
                        ins.then_inc(low_done, 1)
                        pe.wait_ge(low_copied, 1)
                        for h in range(HEADS):
                            if h >= 2:
                                pe.wait_ge(low_biased, h - 1)
                            mm(PS[:, 4 + h % 2, :], A2[:, h * P:(h + 1) * P], GA, start=True, stop=True).then_inc(low_z, 1)
                    elif kind == "proj":
                        name, g = arg
                        bank = PS[:, n % 2, :]
                        s, val = unit_slot(l, ("w", name))
                        if g == 0:
                            pe.wait_ge(unit_in[l][s], val)
                        if n >= 2:
                            pe.wait_ge(taken[n % 2], n // 2)
                        if name == "wo0" and g == 0:
                            for name_ in (("rg", "hg") if l == 0 else ("gg0", "gg1")):
                                for g_ in (2, 3):
                                    pe.wait_ge(*took(l, name_, g_))
                        for k in range(KD):
                            if name[0:2] == "wo":
                                lhs, rhs = OT[:, k, g * P:(g + 1) * P], slot[s][:, k, :]
                            elif name in ("rv", "hi", "gv0", "gv1"):
                                lhs, rhs = HT[:, k, g * P:(g + 1) * P], slot[s][:, k, :]
                            else:
                                lhs, rhs = slot[s][:, k, g * P:(g + 1) * P], HT[:, k, :]
                            ins = mm(bank, lhs, rhs, start=k == 0, stop=k == KD - 1)
                        ins.then_inc(proj_done, 1)
                    elif kind == "A":
                        what, h = arg
                        Qs = {"ret": QR, "hg": QH, "gla": QG}[what][:, h, :]
                        Ks = {"ret": KR_[:, h, :], "hg": KB[n % 2], "gla": KG[:, h, :]}[what]
                        Kd = {"ret": KR_, "hg": FH, "gla": LA}[what][:, h, :]
                        pe.wait_ge(qk_ready, n + 1)
                        if n:
                            pe.wait_ge(o_rstd, n)
                            pe.wait_ge(keys_copied, n)
                        for i in range(NT):
                            sl = slice(i * P, (i + 1) * P)
                            ins = mm(PS[:, 2, sl], Ks[:, sl], Qs[:, sl], start=True, stop=True)
                        ins.then_inc(scores_done, 1)
                        for i in range(NT):
                            sl = slice(i * P, (i + 1) * P)
                            ins = nc.tensor.transpose(PS[:, 3, sl], Kd[:, sl], ident)
                        ins.then_inc(keysT_done, 1)
                    elif kind == "B":
                        what, h = arg
                        pe.wait_ge(keys_copied, n + 1)
                        names = {"ret": ("rv",), "hg": ("hi",), "gla": ("gv0", "gv1")}[what]
                        for name in names:
                            for g in (2, 3):
                                pe.wait_ge(*took(l, name, g))
                        fb = fills_before(n)
                        if n:
                            pe.wait_ge(states_ready, fb)
                        V = {"ret": VR, "hg": VH, "gla": VG}[what]
                        width = 256 if what == "gla" else 128
                        for f, cs in enumerate(FILLS[what]):
                            if f:
                                pe.wait_ge(states_ready, fb + f)
                            for j, c_ in enumerate(cs):
                                if what == "ret":
                                    rows, i = slice(0, P), c_
                                else:
                                    rows, i = slice(64 * (c_ % 2), 64 * (c_ % 2) + 64), c_ // 2
                                bank_, col = update_at(what, c_)
                                ins = mm(PS[:, bank_, col:col + width], KTS[rows, i, :],
                                         V[rows, i, h * width:(h + 1) * width], start=True, stop=True)
                            ins.then_inc(u_done, 1)
                    elif kind == "C":
                        what, h = arg
                        pe.wait_ge(masked, n + 1)
                        pe.wait_ge(states_ready, fills_before(n + 1))
                        if n:
                            pe.wait_ge(o_stored, n)
                        if what == "gla" and h == 0:
                            pe.wait_ge(low_copied, 1)
                        V = {"ret": VR, "hg": VH, "gla": VG}[what]
                        mask = SMR if what == "ret" else SM
                        ST = STG if what == "gla" else STH
                        width = 256 if what == "gla" else 128
                        step_ = P if what == "ret" else CHUNK
                        for d in range(width // P):
                            o_ = PS[:, 6 + d, :]
                            for i in range(NT):
                                sl = slice(i * P, (i + 1) * P)
                                mm(o_[:, sl], V[:, i, h * width + d * P:h * width + (d + 1) * P], mask[:, sl],
                                   start=i == 0, stop=False, skip_group_check=True)
                            for c_ in range(1, S // step_):
                                sl = slice(c_ * step_, (c_ + 1) * step_)
                                ins = mm(o_[:, sl], ST[:, c_, d * P:(d + 1) * P], EB[n % 2][:, sl], start=False,
                                         stop=c_ == S // step_ - 1, skip_group_check=True)
                        ins.then_inc(o_done, 1)
                    elif kind == "D":
                        what, h = arg
                        nh = 2 if what == "gla" else 1
                        sq = sum(2 if k >= 2 * HEADS else 1 for k in range(n + 1))
                        pe.wait_ge(o_squared, sq)
                        for d in range(nh):
                            ins = mm(PS[:, 2, :], ones, SQ[:, d, :], start=d == 0, stop=d == nh - 1)
                        ins.then_inc(o_sum, 1)
                    elif kind == "gb":
                        gate_rows(arg[0])
                        rows_made = 2 * arg[0] + 2
                n_ = 2 * l + 1
                ml = m[l]
                to_hT(n_)
                hT_complete(n_)
                pe.wait_ge(cols_in, 32)
                for i in range(NT):
                    for k in range(KD):
                        ins = mm(PS[:, 2, i * E:(i + 1) * E], HT[:, k, i * P:(i + 1) * P], WR[:, k, :],
                                 start=k == 0, stop=k == KD - 1)
                ins.then_inc(logits_done, 1)
                pe.wait_ge(picks_ready, l + 1)
                MM = RT[:, 7, :, :]
                for i in range(NT):
                    for j in range(i + 1):
                        mm(PS[:, 3, i * E:(i + 1) * E], K("tri") if j == i else ones, MM[:, j, :],
                           start=j == 0, stop=j == i)
                for j in range(NT):
                    ins = mm(PS[:, 3, NT * E:NT * E + E], ones, MM[:, j, :], start=j == 0, stop=j == NT - 1)
                ins.then_inc(ranks_done, 1)
                gate_rows(n_)
                pe.wait_ge(lists_in, 16 * (l + 1))
                pe.wait_ge(slots_ready, l + 1)
                nc.tensor.transpose(PS[:, 3, 0:NLIST], lists_rows, ident[0:NLIST, 0:NLIST]).then_inc(listsT, 1)
                pe.wait_ge(ctrl_ready, l + 1)
                pairs = pe.value_load(ctrl[0:1, 0:1], min_val=E // 2 - 1, max_val=(E + MAXOVER) // 2 - 1) + 1
                regs = [pe.alloc_register(f"pe{l}_r{k}") for k in range(4)]

                def rows_in_T(b):
                    for k in range(KD):
                        ins = nc.tensor.transpose(PS[:, k // 4, (k % 4) * P:(k % 4 + 1) * P],
                                                  G[b][:, k * P:(k + 1) * P], ident)
                        if k % 4 == 3:
                            ins.then_inc(ml["rowsT_done"], 1)

                pe.wait_ge(ml["rows_gatheredA"], 16)
                rows_in_T(0)
                pe.wait_ge(lists_ready, l + 1)
                pe.wait_ge(gb_ready, 2 * n_ + 2)
                with pe.Fori(0, pairs) as i:
                    i1 = keep(pe, regs[0], i * 16 + 16)
                    i2 = keep(pe, regs[1], i * 2)
                    i4 = keep(pe, regs[2], i * 4)
                    for b in range(2):
                        gate, up, down = slot[3 * b], slot[3 * b + 1], slot_down[3 * b + 2]
                        ab = "AB"[b]
                        pe.wait_ge(ml["gate" + ab], i1)
                        pe.wait_ge(ml["gt_act"], i2 + (b + 1))
                        pe.wait_ge(ml["gt_dve"], i2 + (b + 1))
                        pe.wait_ge(ml["silu_done"], i2 + b)
                        for k in range(KD):
                            ins = mm(PS[:, 2, :], GT[b][:, k, :], gate[:, k, :], start=k == 0, stop=k == KD - 1)
                        ins.then_inc(ml["gate_done"], 1)
                        if b == 0:
                            pe.wait_ge(ml["rows_gatheredB"], i1)
                        else:
                            pe.wait_ge(ml["rows_gatheredA"], i1 + 16)
                        rows_in_T(1 - b)
                        pe.wait_ge(ml["up" + ab], i1)
                        pe.wait_ge(ml["prod_done"], i4 + 2 * b)

                        def products_T(f):
                            for q in (2 * f, 2 * f + 1):
                                ins = nc.tensor.transpose(PS[:, 5, q * P:(q + 1) * P], AA[:, q * P:(q + 1) * P], ident)
                            ins.then_inc(ml["prodT_done"], 1)

                        for k in range(KD):
                            ins = mm(PS[:, 3, 0:256], GT[b][:, k, :], up[:, k, 0:256], start=k == 0, stop=k == KD - 1)
                        ins.then_inc(ml["up_done"], 1)
                        for k in range(KD):
                            if k == 5:
                                pe.wait_ge(ml["prod_done"], i4 + (2 * b + 1))
                                pe.wait_ge(ml["prodT_copied"], i4 + 2 * b)
                                products_T(0)
                            ins = mm(PS[:, 4, 0:256], GT[b][:, k, :], up[:, k, 256:512], start=k == 0, stop=k == KD - 1)
                        ins.then_inc(ml["up_done"], 1)
                        pe.wait_ge(ml["down" + ab], i1)
                        pe.wait_ge(ml["y_ready"], i4 + 2 * b)
                        for f in range(KE):
                            if f == 1:
                                pe.wait_ge(ml["prod_done"], i4 + (2 * b + 2))
                                products_T(1)
                            if f % 2 == 0:
                                pe.wait_ge(ml["prodT_copied"], i4 + (2 * b + f // 2 + 1))
                            for h_ in range(2):
                                ins = mm(PS[:, 6 + h_, :], AT[:, f, :], down[:, f, h_ * 512:h_ * 512 + 512],
                                         start=f == 0, stop=f == KE - 1)
                        ins.then_inc(ml["down_done"], 1)


_INS = ["x", "c", "w_ada", "b_ada", "norm_mix_w", "norm_ffn_w", "w_in_even", "hg_lb_logits", "hg_norm_w",
        "ret_norm_w", "w_out_even", "w_in_odd", "w_gla_a2", "b_gla_a2", "gla_norm_w", "w_out_odd", "w_router",
        "b_router", "w_gate", "w_up", "w_down", "final_norm_w"]


def kernel(**inputs):
    import concourse.bacc as _bacc
    from concourse.bass_utils import run_bass_kernel_spmd as _run

    nc = _bacc.Bacc("TRN2", target_bir_lowering=False, num_devices=1)
    arrays, args = {}, []
    table, mask = constants()
    for name, a in [(n, inputs[n]) for n in _INS] + [("consts", table), ("cmask", mask)]:
        a = np.ascontiguousarray(a)
        arrays[f"in_{name}"] = a
        args.append(nc.dram_tensor(f"in_{name}", a.shape, mybir.dt.from_np(a.dtype), kind="ExternalInput").ap())
    args.append(nc.dram_tensor("out_0", (1, S, D), F32, kind="ExternalOutput").ap())
    trunk(nc, *args)
    r = _run(nc, [arrays], core_ids=[0])
    return r.results[0]["out_0"]
```

```python
from contextlib import ExitStack

import numpy as np

import concourse.bass as bass
from concourse import mybir

F32 = mybir.dt.float32
U32 = mybir.dt.uint32
U8 = mybir.dt.uint8
ALU = mybir.AluOpType
ACT = mybir.ActivationFunctionType
AX = mybir.AxisListType.X

P = 128
D = 1024
S = 512
DEPTH = 2
EPS = 1e-6
NT = S // P
KD = D // P
CHUNK = 64
NCH = S // CHUNK
HEADS = 4
E = 16
GROUPS = 4
EPG = E // GROUPS
DE = D // 2
KE = DE // P
UNIT = 8 * 512
NADA = 6 * D // 512
MAXOVER = 8
NLIST = E + MAXOVER + 2
GLA_RANK = 16
BIG = 100.0
ROUND = 1.5 * 2.0 ** 23

CONST_WIDTHS = [("ident", 128), ("select", 24), ("eps", 1), ("ones", 128), ("tri", 128), ("scanmask", 512),
                ("cos", 512), ("sin", 512),
                ("gamrow", 4 * 128), ("decay", 4 * 128), ("kdecay", 4), ("tokid", 4), ("iota_e", 16),
                ("iota_e_big", 16), ("iota_g_big", 4), ("iota_j", 8)]
CONST_AT = {}
NCONST = 0
for _name, _w in CONST_WIDTHS:
    CONST_AT[_name] = (NCONST, NCONST + _w)
    NCONST += _w
NFIRST = CONST_AT["eps"][1]


def gamma_powers():
    f32 = np.float32
    lg = np.log1p(-np.exp2(f32(-5.0) - np.arange(HEADS, dtype=f32))).astype(f32)
    return lg.astype(np.float64)


def constants():
    f32 = np.float32
    c = np.zeros((P, NCONST), f32)

    def put(name, v):
        a, b = CONST_AT[name]
        c[:, a:b] = v

    p = np.arange(P)
    t = np.arange(S)
    put("ident", np.eye(P))
    put("ones", 1.0)
    put("tri", (p[:, None] < p[None, :]))
    put("scanmask", (t % CHUNK != 0)[None, :])
    half = P // 2
    inv = f32(10000.0) ** (-np.arange(0, P, 2, dtype=f32) / f32(P))
    ang = (np.arange(S, dtype=f32)[:, None] * inv[None, :].astype(f32)).astype(f32)
    put("cos", np.cos(ang).T[p % half])
    put("sin", np.sin(ang).T[p % half] * np.where(p < half, -1.0, 1.0)[:, None])
    lg = gamma_powers()
    scale = float(P) ** -0.5
    put("gamrow", np.concatenate([np.exp(lg[h] * (p + 1)) for h in range(HEADS)])[None, :])
    dist = p[None, :] - p[:, None]
    put("decay", np.concatenate([np.where(dist >= 0, np.exp(lg[h] * dist) * scale, 0.0) for h in range(HEADS)], 1))
    put("kdecay", np.stack([np.exp(lg[h] * (P - 1 - p)) * scale for h in range(HEADS)], 1))
    put("tokid", p[:, None] + P * np.arange(NT)[None, :])
    put("iota_e", np.arange(E)[None, :])
    put("iota_e_big", np.arange(E)[None, :] + BIG)
    put("iota_g_big", np.arange(GROUPS)[None, :] + BIG)
    put("iota_j", np.arange(MAXOVER)[None, :])
    put("eps", EPS)
    put("select", (np.arange(24) == 12)[None, :])
    s = p[:, None]
    tt = p[None, :]
    m = ((s // CHUNK == tt // CHUNK) & (s <= tt)).astype(f32)
    return c, np.tile(m, (1, NT))


ADA_GROUPS = [4, 8, 12]
PE_TILES = [4, 4, 3, 3]
GATES = {"hg": 0, "rg": 4, "gg0": 0, "gg1": 4}


def core_slots(kinds):
    heads = [(k, h) for k in kinds for h in range(HEADS)]
    prep = lambda h: [("prepF", *h), ("prep1", *h), ("prep2", *h)]
    out = [prep(heads[0]), [("A", *heads[0])] + prep(heads[1]), [("B", *heads[0]), ("B2", *heads[0])]]
    for i, h in enumerate(heads):
        nxt = heads[i + 1] if i + 1 < len(heads) else None
        p = prep(heads[i + 2]) if i + 2 < len(heads) else []
        out.append([("C", *h)] + ([("A", *nxt)] if nxt else []))
        out.append(p[0:1] + ([("B", *nxt)] if nxt else []) + [("D", *h)] + ([("B2", *nxt)] if nxt else []) +
                   p[1:2] + [("E", *h)] + p[2:3])
    return out


def needs(step):
    kind, what, h = step
    if kind == "prepF":
        return {"ret": [("rq", h), ("rk", h)], "hg": [("hf", h), ("hq", h)], "gla": [("gq", h), ("gk", h)]}[what]
    if kind == "B":
        return [({"ret": "rv", "hg": "hi", "gla": "gv0" if h < 2 else "gv1"}[what], 3)]
    return []


def gate_head(name, g):
    return {"rg": ("E", "ret", g), "hg": ("E", "hg", g), "gg0": ("E", "gla", g // 2), "gg1": ("E", "gla", 2 + g // 2)}[name]


def schedule():
    phases = []
    for kinds, names, ada in ((("ret", "hg"), ("rq", "rk", "rv", "hi", "hf", "hq", "rg", "hg", "wo0", "wo1"), True),
                              (("gla",), ("gq", "gk", "gv0", "gv1", "gg0", "gg1", "wo0", "wo1"), False)):
        st = []
        nxt = [0]

        if ada:
            for a in range(4):
                st.append(("ada", a))
                st.append(("adacol", a))
                if a >= 1:
                    st += [("st", 0, i) for i in ([], [0, 1], [2, 3], [])[a]]
                if a == 3:
                    st += [("tr", 0, 0), ("tr", 0, 1)]
            st.append(("adaT", 0))
            nxt[0] = 4
            st.append(("am", 0))
            for i in range(NT):
                if i >= 2:
                    st.append(("tr", 0, i))
                st.append(("ht", 0, i))
        core = core_slots(kinds)
        done = set()

        def pop():
            for step in core.pop(0):
                st.append(step)
                done.add(step)

        for name in names:
            if name == "wo0":
                assert not core
                st.append(("gb", 0 if ada else 2))
            for g in range(4):
                if name in GATES:
                    while gate_head(name, g) not in done:
                        pop()
                st.append(("proj", name, g))
                done.add((name, g))
                if name == "gq":
                    st += [[("low", 0)], [("lowz", 0), ("lowz", 1)], [("lowz", 2), ("lowz", 3)], []][g]
                if name == "wo0" and g == 0:
                    st.append(("gb", 1 if ada else 3))
                if core and all(n in done for step in core[0] for n in needs(step)):
                    pop()
                if ada and g == 2 and name == "wo1":
                    st += [("adacol", 2 * NADA - 2), ("adacol", 2 * NADA - 1), ("adaT", 2)]
                if ada and (g % 2 == 1 if name not in ("rq", "wo1") else g < 2):
                    a = nxt[0]
                    nxt[0] += 1
                    if a - 2 >= 4:
                        st.append(("adacol", a - 2))
                        if a - 2 == sum(ADA_GROUPS[:2]) - 1:
                            st.append(("adaT", 1))
                    if a < 2 * NADA:
                        st.append(("ada", a))
                if name == "wo1":
                    n = 3 - 2 * ada
                    if g >= 1:
                        st += [("tr", n, g - 1), ("ht", n, g - 1)]
                    if g >= 2:
                        st.append(("logits", n, g - 2))
                    st.append(("st", n, g))
                if name == names[-3] and g == 2:
                    while core:
                        pop()
                    st.append(("diag", 0 if ada else 2))
                    st += [("diag", 1 if ada else 3), ("am", 1 if ada else 3)]
        n = 3 - 2 * ada
        st += [("logits", n, NT - 2), ("tr", n, NT - 1), ("ht", n, NT - 1), ("logits", n, NT - 1)]
        phases.append(st)
    return phases


def number(phases):
    seen = {}
    out = []
    for st in phases:
        ph = []
        for step in st:
            kind = step[0]
            ph.append((step, seen.get(kind, 0)))
            seen[kind] = seen.get(kind, 0) + 1
        out.append(ph)
    return out


FILLS = {"ret": [[0, 1, 2]], "hg": [[0, 1, 2, 3, 4, 5, 6]], "gla": [[0, 1, 2, 3], [4, 5, 6]]}


def update_at(what, c):
    if what == "gla":
        return 4 + c % 4 // 2, c % 2 * 2 * P
    return 4 + c // 4, c % 4 * P


def fills_before(n):
    return sum(len(FILLS[("ret", "hg", "gla")[h // HEADS]]) for h in range(n))


def rot_index(name, g):
    return g + (HEADS if name == "rk" else 0)


W_COLS = {"hq": 0, "hf": 1, "hi": 2, "hg": 3, "rq": 4, "rk": 5, "rv": 6, "rg": 7,
          "gq": 0, "gk": 1, "gv0": 2, "gv1": 3, "gg0": 4, "gg1": 5}


def ring_units(phases):
    out = []
    for layer, st in enumerate(phases):
        units = []
        for step in st:
            u = ("ada", step[1]) if step[0] == "ada" else ("w", step[1]) if step[0] == "proj" else None
            if u and u not in units:
                units.append(u)
        out.append(units)
    return out


class Chain:

    def __init__(self, eng, sem):
        self.eng, self.sem, self.n = eng, sem, 0

    def add(self, ins):
        ins.then_inc(self.sem, 1)
        self.n += 1

    def wait(self):
        self.eng.wait_ge(self.sem, self.n)

    def link(self, ins):
        self.add(ins)
        self.wait()


def keep(eng, reg, value):
    eng.reg_mov(reg, value)
    return eng.snap(reg)


def trunk(nc, x, c, w_ada, b_ada, norm_mix_w, norm_ffn_w, w_in_even, hg_lb_logits, hg_norm_w, ret_norm_w,
          w_out_even, w_in_odd, w_gla_a2, b_gla_a2, gla_norm_w, w_out_odd, w_router, b_router, w_gate, w_up,
          w_down, final_norm_w, consts, cmask, out):
    phases = number(schedule())
    units = ring_units(schedule())
    gamma = np.exp(gamma_powers() * P)

    with ExitStack() as ctx:
        def sb(name, shape, dt=F32):
            return ctx.enter_context(nc.sbuf_tensor(name, shape, dt))

        def sem(name):
            return ctx.enter_context(nc.semaphore(name))

        def dram(name, shape, dt=F32):
            return nc.dram_tensor(name, shape, dt, kind="Internal").ap()

        ring = sb("ring", [P, 6, UNIT])
        X = sb("X", [P, NT, D])
        HT = sb("HT", [P, KD, S])
        OT = sb("OT", [P, KD, S])
        XN_EVEN = OT[:, :, :].rearrange("p k s -> p (k s)").rearrange("p (t d) -> p t d", t=NT)
        MX = sb("MX", [P, 6 * 2048])
        SC = ring[:, 4:6, :].rearrange("p a b -> p (a b)")
        C = sb("C", [P, NCONST])
        CM = sb("CM", [P, S], U8)
        VC = sb("VC", [P, 168])
        MOD = sb("MOD", [P, 2 * 48])
        AM = sb("AM", [P, 4, KD])
        WR = sb("WR", [P, KD, E])
        BR = sb("BR", [P, E])
        cact = sb("cact", [P, KD])
        lb = sb("lb", [P, 3, 4])
        lbs = sb("lbs", [P, 4, 4])
        stat = sb("stat", [P, 4, NT])
        smal = sb("smal", [P, 2, 4, NCH])
        PS = ctx.enter_context(nc.psum_tensor("PS", [P, 8, 512], F32))

        def K(name):
            a, b = CONST_AT[name]
            return C[:, a:b]

        ident = K("ident")
        ones = K("ones")
        slot = [ring[:, s, :].rearrange("p (k n) -> p k n", k=8) for s in range(6)]
        slot_down = [ring[:, s, :].rearrange("p (k n) -> p k n", k=KE) for s in range(6)]

        at = [0]

        def sc(n):
            at[0] += n
            assert at[0] <= 2 * UNIT
            return SC[:, at[0] - n:at[0]]

        EB = [sc(512), sc(512)]
        BB = sc(512)
        KTS = sc(512).rearrange("p (i n) -> p i n", i=NT)
        SM = sc(512)
        SQ = sc(1024).rearrange("p (a n) -> p a n", a=2)
        RR = sc(512)
        shared = at[0]
        KB = [sc(512), sc(512)]
        SMR = sc(512)
        STH = sc(1024).rearrange("p (c n) -> p c n", c=8)
        SW = sc(512)
        ACC = [sc(512), sc(512)]
        AR = SW
        at[0] = shared
        STG = sc(2048).rearrange("p (c n) -> p c n", c=8)
        KTG = sc(512).rearrange("p (i n) -> p i n", i=NT)
        at[0] = shared
        rows1 = sc(128)
        rows2 = sc(128)

        KTODD = {"hg": SQ[:, 1, :].rearrange("p (i n) -> p i n", i=NT), "gla": KTG}

        def mx(k, n=1):
            return MX[:, k * 512:(k + n) * 512]

        def four(k):
            return MX[:, k * 512:(k + 4) * 512].rearrange("p (h n) -> p h n", h=4)

        FH, QH, VH, QR, KR_, VR = four(0), four(4), four(8), four(12), four(16), four(20)
        QG, KG, LA = four(0), four(4), four(16)
        VG = MX[:, 8 * 512:16 * 512].rearrange("p (t n) -> p t n", t=NT)
        A2 = MX[0:GLA_RANK, 20 * 512:21 * 512]
        GA = MX[0:GLA_RANK, 21 * 512:22 * 512]
        WT = MX[:, 22 * 512:22 * 512 + KD * GLA_RANK].rearrange("p (k n) -> p k n", k=KD)
        GBM, DGM = mx(20, 2), mx(22, 2)
        GBE, DGE = mx(0, 2), mx(2, 2)
        JT = mx(4)
        LT = MX[0:E, 4 * 512:5 * 512]
        JUNK = mx(13, 2)
        FW = mx(22, 2)
        XN = [XN_EVEN, mx(5, 8).rearrange("p (t d) -> p t d", t=NT)]
        CZ = mx(20)[:, 0:7 * KD].rearrange("p (k n) -> p k n", k=KD)
        HOT = [mx(16).rearrange("p (i n) -> p i n", i=NT), mx(17).rearrange("p (i n) -> p i n", i=NT)]
        COUNT = mx(15)[:, 0:P]
        G = [mx(5, 2), mx(7, 2)]
        GT = [mx(9, 2).rearrange("p (k n) -> p k n", k=KD), mx(11, 2).rearrange("p (k n) -> p k n", k=KD)]
        SG = mx(13)
        AA = mx(14)
        AT = mx(15).rearrange("p (k n) -> p k n", k=KE)
        Y = [mx(16, 2), mx(18, 2)]
        YG = [[mx(5, 2), mx(7, 2)], [mx(9, 2), mx(11, 2)], [mx(0, 2), mx(2, 2)], [mx(15, 2), mx(17, 2)]]
        RT = MX[:, 20 * 512:24 * 512].rearrange("p (n i e) -> p n i e", n=32, i=NT)
        ZERO = mx(22, 2)
        CMF = mx(8)
        small = sb("small", [P, 12, NT])
        slots = sb("slots", [P, 2, NT], U32)
        places = sb("places", [P, 2, NT], U32)
        rowt = sb("rowt", [P, 8, E])
        ctrlf = sb("ctrlf", [P, 2 + NLIST])
        ctrl = sb("ctrl", [P, 2 + NLIST], U32)
        lists = sb("lists", [P, NLIST])
        cur = sb("cur", [P, 2], U32)
        start = sb("start", [P, 1])

        xn_dram = [dram(f"xn_dram{l}", [S, D]) for l in range(DEPTH)]
        start_dram = dram("start_dram", [DEPTH, 2, P, 1])
        y_dram = dram("y_dram", [(E + MAXOVER) * P, D])
        list_dram = [dram(f"list_dram{l}", [P * NLIST, 1]) for l in range(DEPTH)]

        consts_in = sem("consts_in")
        x_in = sem("x_in")
        rows_in = sem("rows_in")
        cols_in = sem("cols_in")
        lists_zeroed = sem("lists_zeroed")
        zero_set = sem("zero_set")
        unit_in = [[sem(f"unit_in{l}_{s}") for s in range(4)] for l in range(DEPTH)]
        tail_in = sem("tail_in")
        fw_in = sem("fw_in")
        out_done = sem("out_done")
        dve_step = sem("dve_step")
        act_step = sem("act_step")
        rowsT = sem("rowsT")
        rows_copied = sem("rows_copied")
        c_ready = sem("c_ready")
        lbmax_ready = sem("lbmax_ready")
        lbexp_ready = sem("lbexp_ready")
        ada_acc = sem("ada_acc")
        ada_col = sem("ada_col")
        ada_copied = sem("ada_copied")
        ada_T = sem("ada_T")
        am_ready = sem("am_ready")
        keys_zeroed = sem("keys_zeroed")
        logitsT_done = sem("logitsT_done")
        logitsT_copied = sem("logitsT_copied")
        ada_stored = sem("ada_stored")
        firsts_in = sem("firsts_in")
        cz_ready = sem("cz_ready")
        root_ready = sem("root_ready")
        hot_ready = sem("hot_ready")
        first_ids = sem("first_ids")
        first_rows = sem("first_rows")
        xn_ready = sem("xn_ready")
        hT_psum = sem("hT_psum")
        hT_act = sem("hT_act")
        hT_dve = sem("hT_dve")
        proj_done = sem("proj_done")
        gate_silu = sem("gate_silu")
        taken = [sem("taken0"), sem("taken1")]
        rotated = sem("rotated")
        fin_ready = sem("fin_ready")
        low_done = sem("low_done")
        low_copied = sem("low_copied")
        low_z = sem("low_z")
        low_biased = sem("low_biased")
        low_ln = sem("low_ln")
        f_ready = sem("f_ready")
        lnf_ready = sem("lnf_ready")
        mid_ready = sem("mid_ready")
        exp_ready = sem("exp_ready")
        qk_ready = sem("qk_ready")
        scores_done = sem("scores_done")
        keysT_done = sem("keysT_done")
        masked = sem("masked")
        keys_copied = sem("keys_copied")
        u_done = sem("u_done")
        states_ready = sem("states_ready")
        o_done = sem("o_done")
        o_squared = sem("o_squared")
        o_sum = sem("o_sum")
        o_rstd = sem("o_rstd")
        o_stored = sem("o_stored")
        diag_ready = sem("diag_ready")
        gb_psum = sem("gb_psum")
        gb_ready = sem("gb_ready")
        logits_done = sem("logits_done")
        logits_shifted = sem("logits_shifted")
        logits_exp = sem("logits_exp")
        picks_ready = sem("picks_ready")
        ranks_done = sem("ranks_done")
        slots_ready = sem("slots_ready")
        ctrl_ready = sem("ctrl_ready")
        xn_stored = sem("xn_stored")
        ids_scattered = sem("ids_scattered")
        lists_in = sem("lists_in")
        m = []
        for l in range(DEPTH):
            names = ("gateA upA downA gateB upB downB rows_gatheredA rows_gatheredB rowsT_done gt_act gt_dve "
                     "gate_done up_done silu_done prod_done prodT_done prodT_copied down_done y_ready y_storedA "
                     "y_storedB cur_set").split()
            m.append({n: sem(f"{n}{l}") for n in names})
        yg_in = [sem(f"yg_in{b}") for b in range(2 * NT)]
        x_tile = sem("x_tile")

        block = ctx.enter_context(nc.Block())

        def unit_slot(layer, key):
            n = units[layer].index(key)
            return n % 4, 16 * (n // 4 + 1)

        def expert_rows(w, l, e, rows):
            flat = w.rearrange("l e r n -> (l e r) n")
            base = e * rows + l * E * rows
            return flat[bass.ds(base, rows), :].rearrange("(k p) n -> p k n", p=P)

        ADA_SRC = [w_ada[a // NADA, :, (a % NADA) * 512:(a % NADA) * 512 + 512].rearrange("(k p) n -> p k n", p=P)
                   for a in range(DEPTH * NADA)]

        def unit_source(layer, key):
            if key[0] == "ada":
                return ADA_SRC[key[1]]
            name = key[1]
            if name.startswith("wo"):
                w = (w_out_even if layer == 0 else w_out_odd)[0]
                col = int(name[2])
            else:
                w = (w_in_even if layer == 0 else w_in_odd)[0]
                col = W_COLS[name]
            return w[:, col * 512:col * 512 + 512].rearrange("(k p) n -> p k n", p=P)

        ACT_TILES = [4, 4, 6, 4]

        def hT_at(n, i, k):
            bank = 4 if i % 2 == 0 else 2
            if k >= ACT_TILES[n]:
                bank += 1
            elif k >= 4:
                bank = 6 + i % 2
            return PS[:, bank, k % 4 * P:(k % 4 + 1) * P]

        def used_after(layer, key):
            last = None
            for step, n in phases[layer]:
                if key[0] == "ada" and step == ("ada", key[1]):
                    last = (ada_acc, n + 1) if n >= ADA_GROUPS[0] else (ada_col, n + 1)
                if key[0] == "w" and step[0] == "proj" and step[1] == key[1]:
                    last = (proj_done, n + 1)
            return last

        LAST_CORE = [8, 12]
        EXPERT = [("gateA", w_gate, D, 0, 0), ("upA", w_up, D, 0, 1), ("downA", w_down, DE, 0, 2),
                  ("gateB", w_gate, D, 1, 3), ("upB", w_up, D, 1, 4), ("downB", w_down, DE, 1, 5)]

        @block.sync
        def _(sp):
            regs = [sp.alloc_register(f"sp_r{k}") for k in range(9)]
            last_pair = odd = None
            for l in range(DEPTH):
                order = list(range(len(units[l]))) if l == 0 else [3, 0, 1, 2] + list(range(4, len(units[l])))
                for n in order:
                    key = units[l][n]
                    if n == 2 and l == 1:
                        sp.wait_ge(x_tile, 2 * NT)
                    if n == 1 and l == 0:
                        sp.wait_ge(rows_in, 16 * 9)
                    if n == 2 and l == 0:
                        sp.dma_start(X[:, :, :], x[0].rearrange("(t p) d -> p t d", p=P)).then_inc(x_in, 16)
                    if n == 4 and l == 1:
                            sp.wait_ge(x_tile, 2 * NT)
                            sp.dma_start(WT, w_in_odd[0, :, 6 * 512:6 * 512 + GLA_RANK].rearrange("(k p) n -> p k n", p=P)
                                         ).then_inc(tail_in, 16)
                            sp.dma_start(A2, w_gla_a2[0]).then_inc(tail_in, 16)
                    if n >= 4:
                        sp.wait_ge(*used_after(l, units[l][n - 4]))
                    elif l == 1:
                        s_, v = ((m[0]["gate_done"], last_pair * 2 + odd * 2 + 1),
                                 (m[0]["up_done"], last_pair * 4 + odd * 4 + 2),
                                 (m[0]["down_done"], last_pair * 2 + odd * 2 + 1),
                                 (m[0]["gate_done"], last_pair * 2 + 2))[n]
                        v = keep(sp, regs[8], v)
                        sp.wait_ge(s_, v)
                    s, _v = unit_slot(l, key)
                    sp.dma_start(slot[s], unit_source(l, key)).then_inc(unit_in[l][s], 16)
                for name, w, rows, b, s in EXPERT:
                    if s < 4:
                        n = [k for k in range(len(units[l])) if k % 4 == s][-1]
                        sp.wait_ge(*used_after(l, units[l][n]))
                    else:
                        sp.wait_ge(o_stored, LAST_CORE[l])
                        sp.wait_ge(ada_stored, len(ADA_GROUPS))
                    view = slot_down[s] if rows == DE else slot[s]
                    sp.dma_start(view, expert_rows(w, l, b, rows)).then_inc(m[l][name], 16)
                sp.wait_ge(ctrl_ready, l + 1)
                last_pair = sp.value_load(ctrl[0:1, 0:1], min_val=E // 2 - 1, max_val=(E + MAXOVER) // 2 - 1)
                odd = sp.value_load(ctrl[0:1, 1:2], min_val=0, max_val=1)
                odd_reg = sp.alloc_register(f"sp_odd{l}")
                sp.reg_mov(odd_reg, odd)
                if l == 1:
                    sp.wait_ge(gb_ready, 3)
                    sp.dma_start(FW, final_norm_w.rearrange("(o n) -> o n", o=1).to_broadcast([P, D])).then_inc(fw_in, 16)

                def weights(i0, b):
                    expert = sp.value_load(ctrl[0:1, bass.ds(i0 * 2 + (4 + b), 1)], min_val=0, max_val=E - 1)
                    vals = [keep(sp, regs[3 * b], i0 * 2 + (b + 1)), keep(sp, regs[3 * b + 1], i0 * 4 + (2 * b + 2))]
                    for (name, w, rows, _, s), (done, v) in zip(
                            EXPERT[3 * b:3 * b + 3],
                            ((m[l]["gate_done"], vals[0]), (m[l]["up_done"], vals[1]), (m[l]["down_done"], vals[0]))):
                        src = expert_rows(w, l, expert, rows)
                        sp.wait_ge(done, v)
                        view = slot_down[s] if rows == DE else slot[s]
                        sp.dma_start(view, src).then_inc(m[l][name], 16)

                with sp.Fori(0, last_pair) as i0:
                    for b in range(2):
                        weights(i0, b)
                with sp.If_ne(odd_reg, 0):
                    weights(last_pair, 0)

        @block.gpsimd
        def _(pool):
            regs = [pool.alloc_register(f"pool_r{k}") for k in range(6)]
            nc.gpsimd.memset(ZERO, 0.0).then_inc(zero_set, 1)
            pool.wait_ge(zero_set, 1)
            for l in range(DEPTH):
                pool.dma_start(list_dram[l].rearrange("(p c) o -> p (c o)", p=P), ZERO[:, 0:NLIST]
                               ).then_inc(lists_zeroed, 16)
            pool.wait_ge(proj_done, 1)
            for k in range(E, E + MAXOVER):
                pool.dma_start(y_dram[k * P:(k + 1) * P, :], ZERO).then_inc(lists_zeroed, 16)
            for l in range(DEPTH):
                ml = m[l]
                pool.wait_ge(consts_in, 32)
                for b in range(2):
                    pool.dma_start(start_dram[l, b], K("tokid")[:, 0:1]
                                   ).then_inc(ml["y_storedA" if b == 0 else "y_storedB"], 16)

                def gather(b):
                    pool.indirect_dma_start(G[b], None, xn_dram[l],
                                            bass.IndirectOffsetOnAxis(ap=cur[:, b:b + 1], axis=0)
                                            ).then_inc(ml["rows_gatheredA" if b == 0 else "rows_gatheredB"], 16)

                pool.wait_ge(xn_stored, 16 * NT * (l + 1))
                for b in range(2):
                    pool.wait_ge(first_rows, 2 * l + b + 1)
                    gather(b)
                pool.wait_ge(lists_zeroed, 16 * (DEPTH + MAXOVER))
                pool.wait_ge(slots_ready, l + 1)
                tok = K("tokid")
                for i in range(NT):
                    for k in range(2):
                        pool.indirect_dma_start(list_dram[l], bass.IndirectOffsetOnAxis(ap=places[:, k, i:i + 1], axis=0),
                                                tok[:, i:i + 1], None).then_inc(ids_scattered, 16)
                pool.wait_ge(ids_scattered, 16 * 8 * (l + 1))
                pool.dma_start(lists[:, :], list_dram[l].rearrange("(p c) o -> p (c o)", p=P)).then_inc(lists_in, 16)
                pool.wait_ge(ctrl_ready, l + 1)
                pairs = pool.value_load(ctrl[0:1, 0:1], min_val=E // 2 - 1, max_val=(E + MAXOVER) // 2 - 1) + 1
                odd = pool.value_load(ctrl[0:1, 1:2], min_val=0, max_val=1)
                odd_reg = pool.alloc_register(f"pool_odd{l}")
                pool.reg_mov(odd_reg, odd)

                def one_list(i, b):
                    r_tr = keep(pool, regs[0], i * 4 + (2 * b + 2))
                    r_cur = keep(pool, regs[1], i * 2 + (b + 1))
                    r_y = keep(pool, regs[2], i * 4 + (2 * b + 4))
                    r_row = keep(pool, regs[3], i * (2 * P) + b * P)
                    r_col = keep(pool, regs[4], i * 2 + (b + 2))
                    pool.wait_ge(lists_in, 16 * (l + 1))
                    pool.wait_ge(ml["rowsT_done"], r_tr)
                    nc.gpsimd.tensor_copy(cur[:, b:b + 1], lists[:, bass.ds(r_col, 1)]).then_inc(ml["cur_set"], 1)
                    pool.wait_ge(lists_in, 16 * (l + 1))
                    pool.wait_ge(ml["cur_set"], r_cur)
                    gather(b)
                    pool.wait_ge(lists_in, 16 * (l + 1))
                    pool.wait_ge(ml["y_ready"], r_y)
                    pool.dma_start(y_dram[bass.ds(r_row, P), :], Y[b]
                                   ).then_inc(ml["y_storedA" if b == 0 else "y_storedB"], 16)

                with pool.Fori(0, pairs) as i:
                    for b in range(2):
                        one_list(i, b)
                with pool.If_ne(odd_reg, 0):
                    one_list(pairs, 0)
                more_a = keep(pool, regs[0], pairs * 16 + odd * 16 + 16)
                more_b = keep(pool, regs[1], pairs * 16 + 16)
                more4 = keep(pool, regs[2], pairs * 4 + odd * 2 + 2)
                pool.wait_ge(slots_ready, l + 1)
                pool.wait_ge(ml["y_storedA"], more_a)
                pool.wait_ge(ml["y_storedB"], more_b)
                pool.wait_ge(ml["rows_gatheredA"], more_a)
                pool.wait_ge(ml["rows_gatheredB"], more_b)
                pool.wait_ge(ml["rowsT_done"], more4)
                for i in range(NT):
                    for k in range(2):
                        pool.indirect_dma_start(YG[i][k], None, y_dram,
                                                bass.IndirectOffsetOnAxis(ap=slots[:, k, i:i + 1], axis=0)
                                                ).then_inc(yg_in[2 * i + k], 16)

        @block.scalar
        def _(act):
            me = Chain(act, act_step)
            a = nc.scalar.activation
            act.dma_start(C[:, 0:NFIRST], consts[:, 0:NFIRST]).then_inc(firsts_in, 16)
            rv = lambda t, w: t.rearrange("a (r w) -> (a r) w", w=w)
            act.dma_start(rows1[0:96, :], rv(b_ada, P)).then_inc(rows_in, 16)
            act.dma_start(rows1[96:112, :], rv(norm_mix_w, P)).then_inc(rows_in, 16)
            act.dma_start(rows1[112:128, :], rv(norm_ffn_w, P)).then_inc(rows_in, 16)
            at_ = 0
            for t in (c, hg_lb_logits, hg_norm_w, ret_norm_w, b_gla_a2, gla_norm_w):
                r = t.shape[0] * t.shape[1] // P
                act.dma_start(rows2[at_:at_ + r, :], rv(t, P)).then_inc(rows_in, 16)
                at_ += r
            act.wait_ge(rows_copied, 1)
            a(cact[:, :], VC[:, 128:136], ACT.Silu).then_inc(c_ready, 1)
            act.wait_ge(lbmax_ready, 1)
            a(lb[:, :, :], lb[:, :, :], ACT.Exp).then_inc(lbexp_ready, 1)

            def row_norm(n, i):
                if n == 0:
                    act.wait_ge(x_in, 16)
                else:
                    act.wait_ge(x_tile, NT * (n - 1) + i + 1)
                me.link(a(JUNK, X[:, i, :], ACT.Square, accum_out=stat[:, 0, i:i + 1]))
                a(stat[:, 1, i:i + 1], stat[:, 0, i:i + 1], ACT.Sqrt, bias=K("eps"), scale=1.0 / D).then_inc(root_ready, 1)

            def to_hT(n, i):
                shift = (n // 2) * 48 + (n % 2) * 24
                if n % 2:
                    act.wait_ge(xn_ready, NT * n + i + 1)
                    act.dma_start(xn_dram[n // 2][i * P:(i + 1) * P, :], XN[1][:, i, :]).then_inc(xn_stored, 16)
                act.wait_ge(am_ready, n + 1)
                act.wait_ge(hT_psum, NT * n + i + 1)
                for k in range(ACT_TILES[n]):
                    ins = a(HT[:, k, i * P:(i + 1) * P], hT_at(n, i, k), ACT.Identity,
                            bias=MOD[:, shift + k:shift + k + 1], scale=AM[:, n, k:k + 1])
                ins.then_inc(hT_act, 1)

            def gate_rows(n):
                act.wait_ge(gb_psum, n + 1)
                GB = GBM if n % 2 == 0 else GBE
                for half in range(2):
                    ins = a(GB[:, half * 512:half * 512 + 512], PS[:, 4 + half, :], ACT.Copy)
                    if half == 0:
                        me.add(ins)
                ins.then_inc(gb_ready, 1)

            for l in range(DEPTH):
                for (kind, *arg), n in phases[l]:
                    if kind == "st":
                        row_norm(*arg)
                        if tuple(arg) == (0, NT - 1):
                            act.dma_start(C[:, NFIRST:], consts[:, NFIRST:]).then_inc(consts_in, 16)
                            act.dma_start(CMF, cmask).then_inc(consts_in, 16)
                            act.dma_start(WR[:, :, :], w_router.rearrange("(k p) n -> p k n", p=P)).then_inc(cols_in, 16)
                            act.dma_start(BR[:, :], b_router.rearrange("(o n) -> o n", o=1).to_broadcast([P, E])
                                          ).then_inc(cols_in, 16)
                    elif kind == "ht":
                        to_hT(*arg)
                    elif kind == "adaT":
                        g_ = arg[0]
                        if g_:
                            act.wait_ge(rotated, 2 * HEADS)
                        act.wait_ge(ada_col, sum(ADA_GROUPS[:g_ + 1]))
                        a(AR[0:ADA_GROUPS[g_], :], PS[0:ADA_GROUPS[g_], 7, :], ACT.Copy).then_inc(ada_copied, 1)
                    elif kind == "low":
                        act.wait_ge(low_done, 1)
                        a(GA, PS[0:GLA_RANK, 7, :], ACT.Copy).then_inc(low_copied, 1)
                    elif kind == "lowz":
                        act.wait_ge(low_biased, arg[0] + 1)
                        me.link(a(EB[0], EB[0], ACT.Abs))
                        me.link(a(EB[0], EB[0], ACT.Exp, scale=-1.0))
                        a(EB[0], EB[0], ACT.Ln, bias=1.0).then_inc(low_ln, 1)
                    elif kind == "proj":
                        name, g = arg
                        bank = PS[:, n % 2, :]
                        if name in ("rq", "rk"):
                            dst = QR if name == "rq" else KR_
                            ri = rot_index(name, g)
                            act.wait_ge(proj_done, n + 1)
                            if ri:
                                act.wait_ge(rotated, ri)
                            me.add(a(dst[:, g, :], bank, ACT.Copy))
                            me.add(a(SW[64:128, :], bank[0:64, :], ACT.Copy))
                            a(SW[0:64, :], bank[64:128, :], ACT.Copy).then_inc(taken[n % 2], 1)
                        elif name in ("hf", "hq"):
                            act.wait_ge(proj_done, n + 1)
                            a((FH if name == "hf" else QH)[:, g, :], bank, ACT.Sigmoid).then_inc(taken[n % 2], 1)
                        elif name in GATES:
                            act.wait_ge(proj_done, n + 1)
                            a(bank, bank, ACT.Silu).then_inc(gate_silu, 1)
                        elif name in ("gq", "gk"):
                            act.wait_ge(proj_done, n + 1)
                            a((QG if name == "gq" else KG)[:, g, :], bank, ACT.Copy).then_inc(taken[n % 2], 1)
                    elif kind == "prepF" and arg[0] == "hg":
                        h = arg[1]
                        act.wait_ge(f_ready, h + 1)
                        a(FH[:, h, :], FH[:, h, :], ACT.Ln).then_inc(lnf_ready, 1)
                    elif kind == "prep1" and arg[0] != "ret":
                        what, h = arg
                        b = n % 2
                        F = FH if what == "hg" else LA
                        act.wait_ge(mid_ready, n - HEADS + 1)
                        act.wait_ge(o_done, n - 1)
                        me.add(a(EB[b], F[:, h, :], ACT.Exp))
                        for r in (1, 2, 3):
                            me.add(a(smal[:, b, r, :], smal[:, b, 0 if r == 1 else r, :], ACT.Exp))
                        me.wait()
                        a(F[:, h, :], F[:, h, :], ACT.Exp, scale=-1.0).then_inc(exp_ready, 1)
                    elif kind == "A":
                        what, h = arg
                        act.wait_ge(keysT_done, n + 1)
                        ps = PS[:, 3, :].rearrange("p (i n) -> p i n", i=NT)
                        if what == "ret":
                            a(KTS, ps, ACT.Copy, scale=K("kdecay")[:, h:h + 1]).then_inc(keys_copied, 1)
                        else:
                            act.wait_ge(keys_zeroed, 1 if what == "hg" else 2)
                            me.add(a(KTS[0:64, :, :], ps[0:64, :, :], ACT.Copy))
                            a(KTODD[what][64:128, :, :], ps[64:128, :, :], ACT.Copy).then_inc(keys_copied, 1)
                    elif kind == "C":
                        what, h = arg
                        nh = 2 if what == "gla" else 1
                        act.wait_ge(o_done, n + 1)
                        for d in range(nh):
                            a(SQ[:, d, :], PS[:, 6 + d, :], ACT.Square).then_inc(o_squared, 1)
                    elif kind == "D":
                        what, h = arg
                        dv = 256 if what == "gla" else 128
                        act.wait_ge(o_sum, n + 1)
                        me.link(a(RR, PS[:, 2, :], ACT.Ln, bias=K("eps"), scale=1.0 / dv))
                        a(RR, RR, ACT.Exp, scale=-0.5).then_inc(o_rstd, 1)
                    elif kind == "gb":
                        gate_rows(arg[0])
                n_ = 2 * l + 1
                ml = m[l]
                a(stat[:, 2, 0:1], K("eps"), ACT.Exp)
                act.wait_ge(logitsT_done, l + 1)
                a(LT, PS[0:E, 6, :], ACT.Copy).then_inc(logitsT_copied, 1)
                act.wait_ge(logits_shifted, l + 1)
                a(RT[:, 0, :, :], RT[:, 0, :, :], ACT.Exp).then_inc(logits_exp, 1)
                regs = [act.alloc_register(f"act{l}_r{k}") for k in range(4)]
                act.wait_ge(ctrl_ready, l + 1)
                pairs = act.value_load(ctrl[0:1, 0:1], min_val=E // 2 - 1, max_val=(E + MAXOVER) // 2 - 1) + 1
                odd = act.value_load(ctrl[0:1, 1:2], min_val=0, max_val=1)
                odd_reg = act.alloc_register(f"act_odd{l}")
                act.reg_mov(odd_reg, odd)
                shift = l * 48 + 24

                def rows_out(b, v):
                    act.wait_ge(ml["rowsT_done"], v)
                    for k in range(4):
                        ins = a(GT[b][:, k, :], PS[:, 0, k * P:(k + 1) * P], ACT.Identity,
                                bias=MOD[:, shift + k:shift + k + 1], scale=AM[:, n_, k:k + 1])
                    ins.then_inc(ml["gt_act"], 1)

                rows_out(0, 1)

                def one_list(i, b):
                    i2 = keep(act, regs[0], i * 2)
                    i4 = keep(act, regs[1], i * 4)
                    act.wait_ge(ml["gate_done"], i2 + (b + 1))
                    a(SG, PS[:, 2, :], ACT.Silu).then_inc(ml["silu_done"], 1)
                    rows_out(1 - b, i4 + (2 * b + 3))
                    for f in range(2):
                        act.wait_ge(ml["prodT_done"], i4 + (2 * b + f + 1))
                        a(AT[:, 2 * f:2 * f + 2, :],
                          PS[:, 5, f * 256:(f + 1) * 256].rearrange("p (k n) -> p k n", k=2),
                          ACT.Copy).then_inc(ml["prodT_copied"], 1)

                with act.Fori(0, pairs) as i:
                    for b in range(2):
                        one_list(i, b)
                with act.If_ne(odd_reg, 0):
                    one_list(pairs, 0)
                a(stat[:, 2, 1:2], K("eps"), ACT.Sqrt)
                for i in range(NT):
                    row_norm(n_ + 1, i)
                    if l == 0 and i >= 2:
                        to_hT(n_ + 1, i - 2)
                if l == 0:
                    to_hT(n_ + 1, NT - 2)
                    to_hT(n_ + 1, NT - 1)
            for i in range(NT):
                act.wait_ge(fin_ready, i + 1)
                act.dma_start(out[0, i * P:(i + 1) * P, :], XN[0][:, i, :]).then_inc(out_done, 16)
            act.wait_ge(out_done, 16 * NT)

        def took(layer, name, g):
            n = next(k for step, k in phases[layer] if step == ("proj", name, g))
            return taken[n % 2], n // 2 + 1

        @block.vector
        def _(dve):
            me = Chain(dve, dve_step)
            v = nc.vector
            tt, ts, stt = v.tensor_tensor, v.tensor_scalar, v.scalar_tensor_tensor
            dve.wait_ge(rowsT, 1)
            v.tensor_copy(VC[:, :], PS[:, 0, 0:168]).then_inc(rows_copied, 1)
            dve.wait_ge(rows_copied, 1)
            L = VC[:, 136:148].rearrange("p (r h) -> p r h", r=3)
            me.link(tt(lbs[:, 0, :], L[:, 0, :], L[:, 1, :], ALU.max))
            me.link(tt(lbs[:, 1, :], lbs[:, 0, :], L[:, 2, :], ALU.max))
            tt(lb[:, :, :], L, lbs[:, 1:2, :].to_broadcast([P, 3, 4]), ALU.subtract).then_inc(lbmax_ready, 1)
            dve.wait_ge(lbexp_ready, 1)
            me.link(tt(lbs[:, 2, :], lb[:, 0, :], lb[:, 1, :], ALU.add))
            me.link(tt(lbs[:, 3, :], lbs[:, 2, :], lb[:, 2, :], ALU.add))
            me.link(v.reciprocal(lbs[:, 2, :], lbs[:, 3, :]))
            me.link(tt(lbs[:, 0, :], lb[:, 0, :], lbs[:, 2, :], ALU.mult))
            me.link(ts(lbs[:, 1, :], lbs[:, 0, :], -1.0, 1.0, ALU.mult, ALU.add))
            me.link(v.memset(CZ, 0.0))
            dve.wait_ge(c_ready, 1)
            v.tensor_copy(CZ[:, :, 3:4], cact[:, :].unsqueeze(2)).then_inc(cz_ready, 1)

            n_core = 0

            def modulation_scale(n):
                base = (n // 2) * 48 + (n % 2) * 24
                w = VC[:, 96 + 16 * (n % 2) + KD * (n // 2):][:, 0:KD]
                stt(AM[:, n, :], MOD[:, base + KD:base + 2 * KD], 1.0, w, ALU.add, ALU.mult).then_inc(am_ready, 1)

            def to_hT(n, i):
                shift = (n // 2) * 48 + (n % 2) * 24
                dve.wait_ge(am_ready, n + 1)
                dve.wait_ge(hT_psum, NT * n + i + 1)
                for k in range(ACT_TILES[n], KD):
                    ins = ts(HT[:, k, i * P:(i + 1) * P], hT_at(n, i, k),
                             AM[:, n, k:k + 1], MOD[:, shift + k:shift + k + 1], ALU.mult, ALU.add)
                ins.then_inc(hT_dve, 1)

            def row_norm(n, i):
                dve.wait_ge(root_ready, NT * n + i + 1)
                me.link(v.reciprocal(stat[:, 3, i:i + 1], stat[:, 1, i:i + 1]))
                ts(XN[n % 2][:, i, :], X[:, i, :], stat[:, 3, i:i + 1], None, ALU.mult).then_inc(xn_ready, 1)

            def final_norm(i):
                dve.wait_ge(root_ready, NT * 4 + i + 1)
                me.link(v.reciprocal(stat[:, 3, i:i + 1], stat[:, 1, i:i + 1]))
                stt(XN[0][:, i, :], X[:, i, :], stat[:, 3, i:i + 1], FW, ALU.mult, ALU.mult).then_inc(fin_ready, 1)

            def gate_diagonals(n):
                gate = (n // 2) * 48 + (n % 2) * 24 + 16
                DG = DGM if n % 2 == 0 else DGE
                for j in range(KD):
                    ins = ts(DG[:, j * P:(j + 1) * P], ident, MOD[:, gate + j:gate + j + 1], None, ALU.mult)
                    if j < KD - 1:
                        me.add(ins)
                ins.then_inc(diag_ready, 1)

            def decays(F, h, b):
                me.link(v.tensor_tensor_scan(BB, K("scanmask"), F[:, h, :], 0.0, ALU.mult, ALU.add))
                B3 = BB.rearrange("p (c n) -> p c n", c=NCH)
                mid = B3[:, :, CHUNK // 2 - 1:CHUNK // 2]
                me.add(v.tensor_copy(smal[:, b, 0, :].unsqueeze(2), mid))
                me.link(v.tensor_copy(smal[:, b, 3, :].unsqueeze(2), B3[:, :, CHUNK - 1:CHUNK]))
                me.add(tt(smal[:, b, 2, :], smal[:, b, 3, :], smal[:, b, 0, :], ALU.subtract))
                tt(F[:, h, :].rearrange("p (c n) -> p c n", c=NCH), B3, mid.to_broadcast([P, NCH, CHUNK]),
                   ALU.subtract).then_inc(mid_ready, 1)

            def decayed(F, K_, Q, b, qscale):
                c3 = lambda t: t.rearrange("p (c n) -> p c n", c=NCH)
                me.add(stt(Q, Q, qscale, EB[b], ALU.mult, ALU.mult))
                me.link(tt(K_, K_, F, ALU.mult))
                me.add(tt(c3(EB[b]), c3(Q), smal[:, b, 1, :].unsqueeze(2).to_broadcast([P, NCH, CHUNK]), ALU.mult))
                tt(c3(F), c3(K_), smal[:, b, 2, :].unsqueeze(2).to_broadcast([P, NCH, CHUNK]),
                   ALU.mult).then_inc(qk_ready, 1)
                me.wait()

            gates_seen = 0
            for l in range(DEPTH):
                me.link(v.memset(SM, 0.0))
                if l == 0:
                    me.link(v.memset(KTODD["hg"][0:64, :, :], 0.0))
                else:
                    me.link(v.memset(KTODD["gla"][0:64, :, :], 0.0))
                    v.memset(KTS[64:128, :, :], 0.0).then_inc(keys_zeroed, 1)
                for (kind, *arg), n in phases[l]:
                    if kind == "ht":
                        to_hT(*arg)
                        if tuple(arg) == (0, NT - 1):
                            dve.wait_ge(consts_in, 32)
                            me.link(v.tensor_copy(CM[:, :], CMF))
                    elif kind == "st":
                        row_norm(*arg)
                    elif kind == "am":
                        modulation_scale(arg[0])
                    elif kind == "diag":
                        dve.wait_ge(o_done, n_core)
                        gate_diagonals(arg[0])
                    elif kind == "ada":
                        a_ = arg[0]
                        s, val = unit_slot(l, ("ada", a_))
                        dve.wait_ge(unit_in[l][s], val)
                        if a_ >= 2:
                            dve.wait_ge(ada_col, a_ - 1)
                        k0 = PE_TILES[a_] if a_ < ADA_GROUPS[0] else 0
                        for k in range(k0, KD):
                            if k == k0:
                                ins = ts(ACC[a_ % 2], slot[s][:, k, :], cact[:, k:k + 1], None, ALU.mult)
                            else:
                                ins = stt(ACC[a_ % 2], slot[s][:, k, :], cact[:, k:k + 1], ACC[a_ % 2], ALU.mult, ALU.add)
                            if k < KD - 1:
                                me.link(ins)
                        ins.then_inc(ada_acc, 1)
                    elif kind == "adaT":
                        g_ = arg[0]
                        first, count = sum(ADA_GROUPS[:g_]), ADA_GROUPS[g_]
                        dve.wait_ge(ada_T, g_ + 1)
                        cols = slice(4 * first, 4 * (first + count))
                        uj = lambda t: t.rearrange("p (u j) -> p j u", j=4)
                        tt(uj(MOD[:, cols]), PS[:, 7, 0:64].rearrange("p (j u) -> p j u", j=4)[:, :, 0:count],
                           uj(VC[:, cols]), ALU.add).then_inc(ada_stored, 1)
                        dve.wait_ge(ada_stored, g_ + 1)
                    elif kind == "lowz":
                        h = arg[0]
                        z = PS[:, 4 + h % 2, :]
                        bias = VC[:, 156 + h:157 + h]
                        dve.wait_ge(low_z, h + 1)
                        me.add(ts(LA[:, h, :], z, bias, 0.0, ALU.add, ALU.min))
                        ts(EB[0], z, bias, None, ALU.add).then_inc(low_biased, 1)
                        dve.wait_ge(low_ln, h + 1)
                        me.link(tt(LA[:, h, :], LA[:, h, :], EB[0], ALU.subtract))
                        me.link(ts(LA[:, h, :], LA[:, h, :], 1.0 / 16.0, None, ALU.mult))
                    elif kind == "proj":
                        name, g = arg
                        bank = PS[:, n % 2, :]
                        if name in ("rq", "rk"):
                            Q = (QR if name == "rq" else KR_)[:, g, :]
                            dve.wait_ge(taken[n % 2], n // 2 + 1)
                            me.add(tt(Q, Q, K("cos"), ALU.mult))
                            me.link(tt(SW, SW, K("sin"), ALU.mult))
                            tt(Q, Q, SW, ALU.add).then_inc(rotated, 1)
                        elif name in ("rv", "hi", "gv0", "gv1"):
                            dst = {"rv": VR[:, g, :], "hi": VH[:, g, :], "gv0": VG[:, g, 0:512], "gv1": VG[:, g, 512:1024]}
                            dve.wait_ge(proj_done, n + 1)
                            dve.wait_ge(lists_zeroed, 16 * (DEPTH + MAXOVER))
                            v.tensor_copy(dst[name], bank).then_inc(taken[n % 2], 1)
                        elif name in GATES:
                            k = GATES[name] + g
                            w = {"hg": 148 + g, "rg": 152 + g, "gg0": 160 + g, "gg1": 164 + g}[name]
                            gates_seen += 1
                            dve.wait_ge(gate_silu, gates_seen)
                            dve.wait_ge(o_stored, n_core)
                            stt(OT[:, k, :], OT[:, k, :], VC[:, w:w + 1], bank, ALU.mult, ALU.mult
                                ).then_inc(taken[n % 2], 1)
                        elif name in ("wo0", "wo1"):
                            u = int(name[2])
                            dve.wait_ge(proj_done, n + 1)
                            dve.wait_ge(gb_ready, 2 * l + 1)
                            if u == 1 and g:
                                dve.wait_ge(x_tile, 2 * NT * l + g)
                            else:
                                me.wait()
                            tt(JT, bank, GBM[:, u * 512:u * 512 + 512], ALU.mult).then_inc(taken[n % 2], 1)
                            dve.wait_ge(taken[n % 2], n // 2 + 1)
                            xs = X[:, g, u * 512:u * 512 + 512]
                            ins = tt(xs, xs, JT, ALU.add)
                            if u == 1:
                                ins.then_inc(x_tile, 1)
                            else:
                                me.add(ins)
                    elif kind == "prepF":
                        what, h = arg
                        if n >= 2:
                            dve.wait_ge(o_done, n - 1)
                        if what == "ret":
                            dve.wait_ge(rotated, rot_index("rk", h) + 1)
                        elif what == "hg":
                            F = FH[:, h, :]
                            dve.wait_ge(*took(0, "hf", h))
                            dve.wait_ge(*took(0, "hq", h))
                            me.link(ts(F, F, lbs[:, 1, h:h + 1], lbs[:, 0, h:h + 1], ALU.mult, ALU.add))
                            ts(KB[n % 2], F, -1.0, 1.0, ALU.mult, ALU.add).then_inc(f_ready, 1)
                        else:
                            dve.wait_ge(*took(1, "gq", h))
                            dve.wait_ge(*took(1, "gk", h))
                    elif kind == "prep1":
                        what, h = arg
                        if what == "hg":
                            dve.wait_ge(lnf_ready, h + 1)
                            decays(FH, h, n % 2)
                        elif what == "gla":
                            decays(LA, h, n % 2)
                    elif kind == "prep2":
                        what, h = arg
                        b = n % 2
                        if what == "ret":
                            gr = K("gamrow")[:, h * P:(h + 1) * P].unsqueeze(1).to_broadcast([P, NT, P])
                            tt(EB[b].rearrange("p (i n) -> p i n", i=NT), QR[:, h, :].rearrange("p (i n) -> p i n", i=NT),
                               gr, ALU.mult).then_inc(qk_ready, 1)
                        else:
                            dve.wait_ge(exp_ready, n - HEADS + 1)
                            if what == "hg":
                                decayed(FH[:, h, :], KB[b], QH[:, h, :], b, 1.0)
                            else:
                                decayed(LA[:, h, :], KG[:, h, :], QG[:, h, :], b, float(P) ** -0.5)
                    elif kind == "A":
                        what, h = arg
                        if (what, h) == ("hg", 0):
                            dve.wait_ge(u_done, fills_before(n))
                            v.memset(KTS[64:128, :, :], 0.0).then_inc(keys_zeroed, 1)
                        dve.wait_ge(scores_done, n + 1)
                        if what == "ret":
                            i3 = lambda t: t.rearrange("p (i n) -> p i n", i=NT)
                            dec = K("decay")[:, h * P:(h + 1) * P].unsqueeze(1).to_broadcast([P, NT, P])
                            tt(i3(SMR), i3(PS[:, 2, :]), dec, ALU.mult).then_inc(masked, 1)
                        else:
                            v.copy_predicated(SM, CM[:, :], PS[:, 2, :]).then_inc(masked, 1)
                    elif kind in ("B", "B2"):
                        what, h = arg
                        b = n % 2
                        fills = FILLS[what]
                        ST = STG if what == "gla" else STH
                        width = 256 if what == "gla" else 128
                        fb = fills_before(n)
                        f = int(kind == "B2")
                        if f == len(fills):
                            continue
                        cs = fills[f]
                        dve.wait_ge(u_done, fb + f + 1)
                        for j, c_ in enumerate(cs):
                            bank_, col = update_at(what, c_)
                            u_ = PS[:, bank_, col:col + width]
                            if c_ == 0:
                                ins = v.tensor_copy(ST[:, 1, :], u_)
                            else:
                                dec = float(gamma[h]) if what == "ret" else smal[:, b, 3, c_:c_ + 1]
                                ins = stt(ST[:, c_ + 1, :], ST[:, c_, :], dec, u_, ALU.mult, ALU.add)
                            if j < len(cs) - 1:
                                me.link(ins)
                        ins.then_inc(states_ready, 1)
                        dve.wait_ge(states_ready, fb + f + 1)
                    elif kind == "E":
                        what, h = arg
                        dve.wait_ge(o_rstd, n + 1)
                        nh = 2 if what == "gla" else 1
                        for d in range(nh):
                            k = {"ret": 4 + h, "hg": h, "gla": 2 * h + d}[what]
                            ins = tt(OT[:, k, :], PS[:, 6 + d, :], RR, ALU.mult)
                            if d < nh - 1:
                                me.add(ins)
                        ins.then_inc(o_stored, 1)
                        n_core = n + 1
                n_ = 2 * l + 1
                ml = m[l]
                t = lambda k: RT[:, k, :, :]
                bc = lambda s_: s_.unsqueeze(2).to_broadcast([P, NT, E])
                LG, PR, SEL, TMP, OH1, OH2, SLE, MM, RK = (t(k) for k in range(9))
                red = lambda o, i_, op: v.tensor_reduce(o, i_, AX, op)
                sm_ = lambda k: small[:, k, :]
                dve.wait_ge(logits_done, l + 1)
                dve.wait_ge(cols_in, 32)
                lg = PS[:, 3, 0:NT * E].rearrange("p (i e) -> p i e", i=NT)
                me.link(red(sm_(0), lg, ALU.max))
                tt(LG, lg, bc(sm_(0)), ALU.subtract).then_inc(logits_shifted, 1)
                dve.wait_ge(logits_exp, l + 1)
                me.link(red(sm_(0), LG, ALU.add))
                me.link(v.reciprocal(sm_(1), sm_(0)))
                me.link(tt(PR, LG, bc(sm_(1)), ALU.mult))
                me.link(tt(SEL, PR, BR[:, :].unsqueeze(1).to_broadcast([P, NT, E]), ALU.add))
                g16 = lambda ap: ap.rearrange("p i (g e) -> p (i g) e", g=GROUPS)
                GSC = RT[:, 9, 0, :]
                GEQ = RT[:, 9, 1, :]
                GPN = RT[:, 9, 2, :]
                gi = lambda ap: ap.rearrange("p (i g) -> p i g", i=NT)
                me.link(red(GSC, g16(SEL), ALU.max))
                me.link(red(sm_(2), gi(GSC), ALU.max))
                bg = lambda s_: s_.unsqueeze(2).to_broadcast([P, NT, GROUPS])
                me.link(tt(gi(GEQ), gi(GSC), bg(sm_(2)), ALU.is_ge))
                me.link(stt(gi(GEQ), gi(GEQ), -BIG, K("iota_g_big").unsqueeze(1).to_broadcast([P, NT, GROUPS]),
                            ALU.mult, ALU.add))
                me.link(red(sm_(3), gi(GEQ), ALU.min))
                me.link(tt(gi(GSC), gi(GEQ), bg(sm_(3)), ALU.is_equal))
                me.link(ts(GPN, GSC, -1.0, 1e30, ALU.add, ALU.mult))
                b16 = lambda ap: ap.unsqueeze(2).to_broadcast([P, NT * GROUPS, EPG])
                me.link(tt(g16(SEL), g16(SEL), b16(GSC), ALU.mult))
                me.link(tt(g16(SEL), g16(SEL), b16(GPN), ALU.add))

                def pick(OH, s_):
                    me.link(red(sm_(s_), SEL, ALU.max))
                    me.link(tt(TMP, SEL, bc(sm_(s_)), ALU.is_ge))
                    me.link(stt(TMP, TMP, -BIG, K("iota_e_big").unsqueeze(1).to_broadcast([P, NT, E]), ALU.mult, ALU.add))
                    me.link(red(sm_(s_), TMP, ALU.min))
                    me.link(tt(OH, TMP, bc(sm_(s_)), ALU.is_equal))

                pick(OH1, 4)
                me.link(stt(SEL, OH1, -3e38, SEL, ALU.mult, ALU.add))
                pick(OH2, 5)
                tt(MM, OH1, OH2, ALU.add).then_inc(picks_ready, 1)
                for OH, o_ in ((OH1, 6), (OH2, 7)):
                    me.link(tt(TMP, PR, OH, ALU.mult))
                    me.link(red(sm_(o_), TMP, ALU.add))
                me.link(tt(sm_(8), sm_(6), sm_(7), ALU.add))
                me.link(v.reciprocal(sm_(9), sm_(8)))
                me.add(tt(sm_(6), sm_(6), sm_(9), ALU.mult))
                me.add(tt(sm_(7), sm_(7), sm_(9), ALU.mult))
                me.link(v.tensor_tensor_scan(COUNT, ones, ones, 0.0, ALU.mult, ALU.add))
                dve.wait_ge(ranks_done, l + 1)
                me.link(stt(TMP, PS[:, 3, 0:NT * E].rearrange("p (i e) -> p i e", i=NT), 1.0, MM, ALU.add, ALU.mult))
                for e in range(2):
                    tt(HOT[e], TMP[:, :, e:e + 1].to_broadcast([P, NT, P]),
                       COUNT.unsqueeze(1).to_broadcast([P, NT, P]), ALU.is_equal).then_inc(hot_ready, 1)
                me.add(v.tensor_copy(rowt[:, 0, :], PS[:, 3, NT * E:NT * E + E]))
                me.link(v.tensor_copy(RK, PS[:, 3, 0:NT * E].rearrange("p (i e) -> p i e", i=NT)))
                me.link(ts(rowt[:, 1, :], rowt[:, 0, :], float(P), None, ALU.is_gt))
                me.link(stt(rowt[:, 1, :], rowt[:, 0, :], float(2 * P), rowt[:, 1, :], ALU.is_gt, ALU.add))
                me.link(stt(rowt[:, 1, :], rowt[:, 0, :], float(3 * P), rowt[:, 1, :], ALU.is_gt, ALU.add))
                me.link(v.tensor_tensor_scan(rowt[:, 2, :], ones[:, 0:E], rowt[:, 1, :], 0.0, ALU.mult, ALU.add))
                dve.wait_ge(first_ids, 2 * l + 1)
                v.tensor_copy(cur[:, 0:1], PS[:, 2, 0:1]).then_inc(first_rows, 1)
                me.link(v.memset(ctrlf[:, :], 0.0))
                me.link(v.tensor_copy(ctrlf[:, 2:2 + E], K("iota_e")))
                cmp8 = RT[:, 10:12, :, :].rearrange("p a i e -> p (a i) e")
                me.link(tt(cmp8, rowt[:, 2:3, :].to_broadcast([P, MAXOVER, E]),
                           K("iota_j").unsqueeze(2).to_broadcast([P, MAXOVER, E]), ALU.is_le))
                over = ctrlf[:, 2 + E:2 + E + MAXOVER]
                me.link(red(over, cmp8, ALU.add))
                me.link(ts(over, over, float(E - 1), None, ALU.min))
                total = rowt[:, 2, E - 1:E]
                for k in range(2, MAXOVER, 2):
                    me.link(stt(ctrlf[:, 0:1], total, float(k), ctrlf[:, 0:1], ALU.is_ge, ALU.add))
                me.link(stt(ctrlf[:, 1:2], ctrlf[:, 0:1], -2.0, total, ALU.mult, ALU.add))
                me.link(ts(ctrlf[:, 0:1], ctrlf[:, 0:1], float(E // 2 - 1), None, ALU.add))
                v.tensor_copy(ctrl[:, :], ctrlf[:, :]).then_inc(ctrl_ready, 1)
                dve.wait_ge(first_ids, 2 * l + 2)
                v.tensor_copy(cur[:, 1:2], PS[:, 6, 0:1]).then_inc(first_rows, 1)
                me.link(tt(rowt[:, 3, :], rowt[:, 2, :], rowt[:, 1, :], ALU.subtract))
                me.link(tt(rowt[:, 3, :], rowt[:, 3, :], K("iota_e"), ALU.subtract))
                me.link(ts(rowt[:, 3, :], rowt[:, 3, :], float(E - 1), float(P), ALU.add, ALU.mult))
                me.link(ts(TMP, RK, float(P), None, ALU.is_ge))
                me.link(tt(TMP, TMP, rowt[:, 3:4, :].to_broadcast([P, NT, E]), ALU.mult))
                me.link(tt(SLE, TMP, RK, ALU.add))
                me.link(stt(SLE, K("iota_e").unsqueeze(1).to_broadcast([P, NT, E]), float(P), SLE, ALU.mult, ALU.add))
                for OH, k in ((OH1, 0), (OH2, 1)):
                    me.link(tt(TMP, SLE, OH, ALU.mult))
                    me.link(red(sm_(10 + k), TMP, ALU.add))
                both = small[:, 10:12, :]
                nlist = small[:, 2:4, :]
                me.link(ts(nlist, both, 0.5 - P / 2, 1.0 / P, ALU.add, ALU.mult))
                me.link(ts(nlist, nlist, ROUND, None, ALU.add))
                me.link(ts(nlist, nlist, -ROUND, None, ALU.add))
                me.link(ts(nlist, nlist, float(1 - P * NLIST), None, ALU.mult))
                me.add(v.tensor_copy(slots[:, :, :], both))
                stt(places[:, :, :], both, float(NLIST), nlist, ALU.mult, ALU.add).then_inc(slots_ready, 1)
                dve.wait_ge(ctrl_ready, l + 1)
                pairs = dve.value_load(ctrl[0:1, 0:1], min_val=E // 2 - 1, max_val=(E + MAXOVER) // 2 - 1) + 1
                odd = dve.value_load(ctrl[0:1, 1:2], min_val=0, max_val=1)
                odd_reg = dve.alloc_register(f"dve_odd{l}")
                dve.reg_mov(odd_reg, odd)
                regs = [dve.alloc_register(f"dve{l}_r{k}") for k in range(4)]
                shift = l * 48 + 24

                def rows_out(b, val):
                    dve.wait_ge(ml["rowsT_done"], val)
                    for k in range(4, KD):
                        ins = ts(GT[b][:, k, :], PS[:, 1, (k - 4) * P:(k - 3) * P], AM[:, n_, k:k + 1],
                                 MOD[:, shift + k:shift + k + 1], ALU.mult, ALU.add)
                    ins.then_inc(ml["gt_dve"], 1)

                rows_out(0, 2)
                dve.wait_ge(gb_ready, n_ + 1)
                v.memset(start[:, :], 0.0).then_inc(ml["y_ready"], 2)

                def one_list(i, b):
                    i2 = keep(dve, regs[0], i * 2)
                    i4 = keep(dve, regs[1], i * 4)
                    i16 = keep(dve, regs[2], i * 16 + 16)
                    rows_out(1 - b, i4 + (2 * b + 4))
                    for f in range(2):
                        dve.wait_ge(ml["silu_done"], i2 + (b + 1))
                        dve.wait_ge(ml["up_done"], i4 + (2 * b + f + 1))
                        tt(AA[:, f * 256:(f + 1) * 256], SG[:, f * 256:(f + 1) * 256], PS[:, 3 + f, 0:256],
                           ALU.mult).then_inc(ml["prod_done"], 1)
                    dve.wait_ge(ml["down_done"], i2 + (b + 1))
                    dve.wait_ge(ml["y_storedA" if b == 0 else "y_storedB"], i16)
                    for h_ in range(2):
                        tt(Y[b][:, h_ * 512:h_ * 512 + 512], PS[:, 6 + h_, :], GBE[:, h_ * 512:h_ * 512 + 512],
                           ALU.mult).then_inc(ml["y_ready"], 1)

                with dve.Fori(0, pairs) as i:
                    for b in range(2):
                        one_list(i, b)
                with dve.If_ne(odd_reg, 0):
                    one_list(pairs, 0)
                if l == 0:
                    modulation_scale(n_ + 1)
                else:
                    dve.wait_ge(fw_in, 16)
                for i in range(NT):
                    for k in range(2):
                        dve.wait_ge(yg_in[2 * i + k], 16 * (l + 1))
                        ins = stt(X[:, i, :], YG[i][k], sm_(6 + k)[:, i:i + 1], X[:, i, :], ALU.mult, ALU.add)
                        if k == 0:
                            me.link(ins)
                        else:
                            ins.then_inc(x_tile, 1)
                    if i:
                        if l == 1:
                            final_norm(i - 1)
                        else:
                            row_norm(n_ + 1, i - 1)
                            if i >= 2:
                                to_hT(n_ + 1, i - 2)
                if l == 0:
                    row_norm(n_ + 1, NT - 1)
                    to_hT(n_ + 1, NT - 2)
                    to_hT(n_ + 1, NT - 1)
                else:
                    final_norm(NT - 1)

        @block.tensor
        def _(pe):
            mm = nc.tensor.matmul
            pe.wait_ge(firsts_in, 16)
            pe.wait_ge(rows_in, 16 * 9)
            nc.tensor.transpose(PS[:, 0, 0:128], rows1, ident)
            nc.tensor.transpose(PS[:, 0, 128:168], rows2[0:40, :], ident[0:40, 0:40]).then_inc(rowsT, 1)
            pe.wait_ge(rows_copied, 1)

            def to_hT(n, i):
                pe.wait_ge(xn_ready, NT * n + i + 1)
                if i >= 2:
                    pe.wait_ge(hT_act, NT * n + i - 1)
                    pe.wait_ge(hT_dve, NT * n + i - 1)
                elif n % 2:
                    if i == 0:
                        pe.wait_ge(gb_ready, n + 1)
                    else:
                        pe.wait_ge(o_rstd, LAST_CORE[n // 2])
                        pe.wait_ge(keys_copied, LAST_CORE[n // 2])
                for k in range(KD):
                    ins = nc.tensor.transpose(hT_at(n, i, k),
                                              XN[n % 2][:, i, k * P:(k + 1) * P], ident)
                ins.then_inc(hT_psum, 1)

            def hT_complete(n, i):
                pe.wait_ge(hT_act, NT * n + i + 1)
                pe.wait_ge(hT_dve, NT * n + i + 1)

            def gate_rows(n):
                pe.wait_ge(diag_ready, n + 1)
                if n % 2:
                    pe.wait_ge(gb_ready, n)
                pe.wait_ge(states_ready, fills_before(LAST_CORE[n // 2]))
                DG = DGM if n % 2 == 0 else DGE
                for half in range(2):
                    ins = mm(PS[:, 4 + half, :], ones, DG[:, half * 512:half * 512 + 512], start=True, stop=True)
                ins.then_inc(gb_psum, 1)

            sums, scores = 0, 0
            for l in range(DEPTH):
                for (kind, *arg), n in phases[l]:
                    if kind == "tr":
                        to_hT(*arg)
                    elif kind == "ht":
                        if tuple(arg) == (0, NT - 1):
                            hT_complete(*arg)
                    elif kind == "logits":
                        n_, i = arg
                        hT_complete(n_, i)
                        pe.wait_ge(cols_in, 32)
                        for k in range(KD):
                            ins = mm(PS[0:E, 6, i * P:(i + 1) * P], WR[:, k, :], HT[:, k, i * P:(i + 1) * P],
                                     start=k == 0, stop=k == KD - 1)
                        if i == NT - 1:
                            ins.then_inc(logitsT_done, 1)
                    elif kind == "adacol":
                        a_ = arg[0]
                        g_ = next(g for g in range(3) if a_ < sum(ADA_GROUPS[:g + 1]))
                        r, count = a_ - sum(ADA_GROUPS[:g_]), ADA_GROUPS[g_]
                        if g_:
                            pe.wait_ge(ada_stored, g_)
                        if g_ == 0:
                            pe.wait_ge(cz_ready, 1)
                            s, val = unit_slot(l, ("ada", a_))
                            pe.wait_ge(unit_in[l][s], val)
                            for k in range(PE_TILES[a_]):
                                mm(PS[0:count, 7, :], CZ[:, k, 3 - r:3 - r + count], slot[s][:, k, :],
                                   start=r == 0 and k == 0, stop=False, skip_group_check=True)
                        pe.wait_ge(ada_acc, a_ + 1)
                        mm(PS[0:count, 7, :], K("select")[:, 12 - r:12 - r + count], ACC[a_ % 2],
                           start=r == 0 and g_ > 0, stop=r == count - 1, skip_group_check=True).then_inc(ada_col, 1)
                    elif kind == "adaT":
                        g_ = arg[0]
                        count = ADA_GROUPS[g_]
                        pe.wait_ge(ada_copied, g_ + 1)
                        for j in range(4):
                            ins = nc.tensor.transpose(PS[:, 7, 16 * j:16 * j + count], AR[0:count, j * P:(j + 1) * P],
                                                      ident[0:count, 0:count])
                        ins.then_inc(ada_T, 1)
                    elif kind == "low":
                        pe.wait_ge(tail_in, 32)
                        for k in range(KD):
                            ins = mm(PS[0:GLA_RANK, 7, :], WT[:, k, :], HT[:, k, :], start=k == 0, stop=k == KD - 1)
                        ins.then_inc(low_done, 1)
                    elif kind == "lowz":
                        h = arg[0]
                        pe.wait_ge(low_copied, 1)
                        if h >= 2:
                            pe.wait_ge(low_biased, h - 1)
                        mm(PS[:, 4 + h % 2, :], A2[:, h * P:(h + 1) * P], GA, start=True, stop=True).then_inc(low_z, 1)
                    elif kind == "proj":
                        name, g = arg
                        bank = PS[:, n % 2, :]
                        s, val = unit_slot(l, ("w", name))
                        if g == 0:
                            pe.wait_ge(unit_in[l][s], val)
                        if n >= 2:
                            pe.wait_ge(taken[n % 2], n // 2)
                        if name == "wo0" and g == 0:
                            for name_ in (("rg", "hg") if l == 0 else ("gg0", "gg1")):
                                for g_ in (2, 3):
                                    pe.wait_ge(*took(l, name_, g_))
                        for k in range(KD):
                            if name[0:2] == "wo":
                                lhs, rhs = OT[:, k, g * P:(g + 1) * P], slot[s][:, k, :]
                            elif name in ("rv", "hi", "gv0", "gv1"):
                                lhs, rhs = HT[:, k, g * P:(g + 1) * P], slot[s][:, k, :]
                            else:
                                lhs, rhs = slot[s][:, k, g * P:(g + 1) * P], HT[:, k, :]
                            ins = mm(bank, lhs, rhs, start=k == 0, stop=k == KD - 1)
                        ins.then_inc(proj_done, 1)
                    elif kind == "A":
                        what, h = arg
                        Qs = {"ret": QR, "hg": QH, "gla": QG}[what][:, h, :]
                        Ks = {"ret": KR_[:, h, :], "hg": KB[n % 2], "gla": KG[:, h, :]}[what]
                        Kd = {"ret": KR_, "hg": FH, "gla": LA}[what][:, h, :]
                        pe.wait_ge(qk_ready, n + 1)
                        scores += 1
                        if sums:
                            pe.wait_ge(o_rstd, sums)
                        if n:
                            pe.wait_ge(masked, n)
                            pe.wait_ge(keys_copied, n)
                        for i in range(NT):
                            sl = slice(i * P, (i + 1) * P)
                            ins = mm(PS[:, 2, sl], Ks[:, sl], Qs[:, sl], start=True, stop=True)
                        ins.then_inc(scores_done, 1)
                        for i in range(NT):
                            sl = slice(i * P, (i + 1) * P)
                            ins = nc.tensor.transpose(PS[:, 3, sl], Kd[:, sl], ident)
                        ins.then_inc(keysT_done, 1)
                    elif kind in ("B", "B2"):
                        what, h = arg
                        f = int(kind == "B2")
                        if f == len(FILLS[what]):
                            continue
                        fb = fills_before(n)
                        if f == 0:
                            pe.wait_ge(keys_copied, n + 1)
                            for g in (2, 3):
                                pe.wait_ge(*took(l, needs(("B", what, h))[0][0], g))
                        if fb + f:
                            pe.wait_ge(states_ready, fb + f)
                        V = {"ret": VR, "hg": VH, "gla": VG}[what]
                        width = 256 if what == "gla" else 128
                        for c_ in FILLS[what][f]:
                            if what == "ret":
                                keys, i = KTS, c_
                            else:
                                keys, i = (KTODD[what] if c_ % 2 else KTS), c_ // 2
                            bank_, col = update_at(what, c_)
                            ins = mm(PS[:, bank_, col:col + width], keys[:, i, :],
                                     V[:, i, h * width:(h + 1) * width], start=True, stop=True)
                        ins.then_inc(u_done, 1)
                    elif kind == "C":
                        what, h = arg
                        pe.wait_ge(masked, n + 1)
                        pe.wait_ge(states_ready, fills_before(n + 1))
                        if n:
                            pe.wait_ge(o_stored, n)
                        if what == "gla" and h == 0:
                            pe.wait_ge(low_copied, 1)
                        V = {"ret": VR, "hg": VH, "gla": VG}[what]
                        mask = SMR if what == "ret" else SM
                        ST = STG if what == "gla" else STH
                        width = 256 if what == "gla" else 128
                        step_ = P if what == "ret" else CHUNK
                        for d in range(width // P):
                            o_ = PS[:, 6 + d, :]
                            for i in range(NT):
                                sl = slice(i * P, (i + 1) * P)
                                mm(o_[:, sl], V[:, i, h * width + d * P:h * width + (d + 1) * P], mask[:, sl],
                                   start=i == 0, stop=False, skip_group_check=True)
                            for c_ in range(1, S // step_):
                                sl = slice(c_ * step_, (c_ + 1) * step_)
                                ins = mm(o_[:, sl], ST[:, c_, d * P:(d + 1) * P], EB[n % 2][:, sl], start=False,
                                         stop=c_ == S // step_ - 1, skip_group_check=True)
                        ins.then_inc(o_done, 1)
                    elif kind == "D":
                        what, h = arg
                        nh = 2 if what == "gla" else 1
                        sums += 1
                        pe.wait_ge(masked, scores)
                        sq = sum(2 if k >= 2 * HEADS else 1 for k in range(n + 1))
                        pe.wait_ge(o_squared, sq)
                        for d in range(nh):
                            ins = mm(PS[:, 2, :], ones, SQ[:, d, :], start=d == 0, stop=d == nh - 1)
                        ins.then_inc(o_sum, 1)
                    elif kind == "gb":
                        gate_rows(arg[0])
                n_ = 2 * l + 1
                ml = m[l]
                pe.wait_ge(logitsT_copied, l + 1)
                for i in range(NT):
                    ins = nc.tensor.transpose(PS[:, 3, i * E:(i + 1) * E], LT[:, i * P:(i + 1) * P], ident[0:E, 0:E])
                ins.then_inc(logits_done, 1)
                pe.wait_ge(picks_ready, l + 1)
                MM = RT[:, 7, :, :]
                mm(PS[:, 3, 0:NT * E].rearrange("p (i e) -> p i e", i=NT), K("tri"), MM, start=True, stop=False,
                   skip_group_check=True)
                for j in range(NT):
                    rest = NT - j
                    ins = mm(PS[:, 3, (j + 1) * E:(NT + 1) * E].rearrange("p (i e) -> p i e", i=rest), ones,
                             RT[:, 7, j:j + 1, :].to_broadcast([P, rest, E]), start=False, stop=j == NT - 1,
                             skip_group_check=True)
                ins.then_inc(ranks_done, 1)
                for e in range(2):
                    pe.wait_ge(hot_ready, 2 * l + e + 1)
                    for i in range(NT):
                        ins = mm(PS[:, 2 + 4 * e, 0:1], HOT[e][:, i, :], K("tokid")[:, i:i + 1],
                                 start=i == 0, stop=i == NT - 1)
                    ins.then_inc(first_ids, 1)
                pe.wait_ge(ctrl_ready, l + 1)
                pairs = pe.value_load(ctrl[0:1, 0:1], min_val=E // 2 - 1, max_val=(E + MAXOVER) // 2 - 1) + 1
                odd = pe.value_load(ctrl[0:1, 1:2], min_val=0, max_val=1)
                odd_reg = pe.alloc_register(f"pe_odd{l}")
                pe.reg_mov(odd_reg, odd)
                regs = [pe.alloc_register(f"pe{l}_r{k}") for k in range(4)]

                def rows_in_T(b):
                    for k in range(KD):
                        ins = nc.tensor.transpose(PS[:, k // 4, (k % 4) * P:(k % 4 + 1) * P],
                                                  G[b][:, k * P:(k + 1) * P], ident)
                        if k % 4 == 3:
                            ins.then_inc(ml["rowsT_done"], 1)

                pe.wait_ge(ml["rows_gatheredA"], 16)
                rows_in_T(0)
                pe.wait_ge(slots_ready, l + 1)
                pe.wait_ge(first_rows, 2 * l + 2)
                pe.wait_ge(gb_ready, n_ + 1)

                def one_list(i, b):
                    i1 = keep(pe, regs[0], i * 16 + 16)
                    i2 = keep(pe, regs[1], i * 2)
                    i4 = keep(pe, regs[2], i * 4)
                    gate, up, down = slot[3 * b], slot[3 * b + 1], slot_down[3 * b + 2]
                    ab = "AB"[b]
                    pe.wait_ge(ml["gate" + ab], i1)
                    pe.wait_ge(ml["gt_act"], i2 + (b + 1))
                    pe.wait_ge(ml["gt_dve"], i2 + (b + 1))
                    for k in range(KD):
                        ins = mm(PS[:, 2, :], GT[b][:, k, :], gate[:, k, :], start=k == 0, stop=k == KD - 1)
                    ins.then_inc(ml["gate_done"], 1)
                    if b == 0:
                        pe.wait_ge(ml["rows_gatheredB"], i1)
                    else:
                        pe.wait_ge(ml["rows_gatheredA"], i1 + 16)
                    rows_in_T(1 - b)
                    pe.wait_ge(ml["up" + ab], i1)

                    def products_T(f):
                        for q in (2 * f, 2 * f + 1):
                            ins = nc.tensor.transpose(PS[:, 5, q * P:(q + 1) * P], AA[:, q * P:(q + 1) * P], ident)
                        ins.then_inc(ml["prodT_done"], 1)

                    for k in range(KD):
                        ins = mm(PS[:, 3, 0:256], GT[b][:, k, :], up[:, k, 0:256], start=k == 0, stop=k == KD - 1)
                    ins.then_inc(ml["up_done"], 1)
                    for k in range(KD):
                        if k == 5:
                            pe.wait_ge(ml["prod_done"], i4 + (2 * b + 1))
                            products_T(0)
                        ins = mm(PS[:, 4, 0:256], GT[b][:, k, :], up[:, k, 256:512], start=k == 0, stop=k == KD - 1)
                    ins.then_inc(ml["up_done"], 1)
                    pe.wait_ge(ml["down" + ab], i1)
                    pe.wait_ge(ml["y_ready"], i4 + 2 * b + 2)
                    for f in range(KE):
                        if f == 1:
                            pe.wait_ge(ml["prod_done"], i4 + (2 * b + 2))
                            products_T(1)
                        if f % 2 == 0:
                            pe.wait_ge(ml["prodT_copied"], i4 + (2 * b + f // 2 + 1))
                        for h_ in range(2):
                            ins = mm(PS[:, 6 + h_, :], AT[:, f, :], down[:, f, h_ * 512:h_ * 512 + 512],
                                     start=f == 0, stop=f == KE - 1)
                    ins.then_inc(ml["down_done"], 1)

                with pe.Fori(0, pairs) as i:
                    for b in range(2):
                        one_list(i, b)
                with pe.If_ne(odd_reg, 0):
                    one_list(pairs, 0)
                if l == 0:
                    for i in range(NT):
                        to_hT(n_ + 1, i)
                    hT_complete(n_ + 1, NT - 1)


_INS = ["x", "c", "w_ada", "b_ada", "norm_mix_w", "norm_ffn_w", "w_in_even", "hg_lb_logits", "hg_norm_w",
        "ret_norm_w", "w_out_even", "w_in_odd", "w_gla_a2", "b_gla_a2", "gla_norm_w", "w_out_odd", "w_router",
        "b_router", "w_gate", "w_up", "w_down", "final_norm_w"]


def kernel(**inputs):
    import concourse.bacc as _bacc
    from concourse.bass_utils import run_bass_kernel_spmd as _run

    nc = _bacc.Bacc("TRN2", target_bir_lowering=False, num_devices=1)
    arrays, args = {}, []
    table, mask = constants()
    for name, a in [(n, inputs[n]) for n in _INS] + [("consts", table), ("cmask", mask)]:
        a = np.ascontiguousarray(a)
        arrays[f"in_{name}"] = a
        args.append(nc.dram_tensor(f"in_{name}", a.shape, mybir.dt.from_np(a.dtype), kind="ExternalInput").ap())
    args.append(nc.dram_tensor("out_0", (1, S, D), F32, kind="ExternalOutput").ap())
    trunk(nc, *args)
    r = _run(nc, [arrays], core_ids=[0])
    return r.results[0]["out_0"]
```
